# Optimizing a Trainium2 kernel written in Bass

```python
import jax, jax.numpy as jnp
from jax import lax
import numpy as np

D_MODEL = 2048
BATCH = 1
SEQ = 1024
DEPTH = 1

MEM_LEN = 256
MIX_WIDTH = D_MODEL
A_WIDTH = MIX_WIDTH // 2
A_HEAD_DIM = 128
A_HEADS = A_WIDTH // A_HEAD_DIM
CONV_K = 5
CHUNK = 64
B_WIDTH = MIX_WIDTH // 4
B_HEAD_DIM = 64
B_Q_HEADS = B_WIDTH // B_HEAD_DIM
B_KV_HEADS = B_Q_HEADS // 4
WINDOW = 128
C_WIDTH = MIX_WIDTH // 4
C_HEADS = 4
C_HEAD_DIM = C_WIDTH // C_HEADS

ROPE_THETA = 10000.0
EPS = 1e-6
IN_SIZES = (A_WIDTH, A_WIDTH, A_WIDTH, A_WIDTH, A_HEADS, A_HEADS, A_HEADS, A_HEADS,
            B_WIDTH, B_KV_HEADS * B_HEAD_DIM, B_KV_HEADS * B_HEAD_DIM, B_WIDTH,
            C_WIDTH, C_WIDTH)
IN_WIDTH = sum(IN_SIZES)

kernel_name = "hybrid_deltanet_swa_sink_memxattn_layer"

F32 = jnp.float32

def rms_norm(t, w):
    tf = t.astype(F32)
    y = tf * lax.rsqrt(jnp.mean(tf * tf, axis=-1, keepdims=True) + EPS)
    return (y * w.astype(F32)).astype(t.dtype)

def l2_norm(t):
    tf = t.astype(F32)
    return tf * lax.rsqrt(jnp.sum(tf * tf, axis=-1, keepdims=True) + EPS)

def rope(t):
    seq, d = t.shape[1], t.shape[-1]
    inv = ROPE_THETA ** (-jnp.arange(0, d, 2, dtype=F32) / d)
    ang = jnp.arange(seq, dtype=F32)[:, None] * inv[None, :]
    cos = jnp.cos(ang)[None, :, None, :]
    sin = jnp.sin(ang)[None, :, None, :]
    tf = t.astype(F32)
    t1, t2 = tf[..., : d // 2], tf[..., d // 2:]
    return jnp.concatenate([t1 * cos - t2 * sin, t2 * cos + t1 * sin], axis=-1).astype(t.dtype)

def centred_depthwise_conv(t, w):
    c = t.shape[-1]
    pad = CONV_K // 2
    return lax.conv_general_dilated(
        t, w.astype(t.dtype)[:, None, :], window_strides=(1,), padding=[(pad, pad)],
        dimension_numbers=("NWC", "WIO", "NWC"), feature_group_count=c)

def gated_delta_rule_chunked(q, k, v, g, beta):
    bsz, seq, nh, dk = q.shape
    dv = v.shape[-1]
    n = seq // CHUNK

    def to_chunks(t):
        t = t.astype(F32).reshape((bsz, n, CHUNK, nh) + t.shape[3:])
        return jnp.moveaxis(t, 3, 1)

    q = to_chunks(q) * (dk ** -0.5)
    k, v, g, beta = to_chunks(k), to_chunks(v), to_chunks(g), to_chunks(beta)
    gc = jnp.cumsum(g, axis=-1)
    idx = jnp.arange(CHUNK)
    incl = idx[:, None] >= idx[None, :]
    strict = idx[:, None] > idx[None, :]
    diff = gc[..., :, None] - gc[..., None, :]
    decay = jnp.where(incl, jnp.exp(jnp.where(incl, diff, 0.0)), 0.0)
    kb = k * beta[..., None]
    vb = v * beta[..., None]
    a = -jnp.where(strict, jnp.einsum('bhncd,bhnkd->bhnck', kb, k) * decay, 0.0)

    def fwd_sub(i, tm):
        row = tm[..., i, :]
        return tm.at[..., i, :].set(row + jnp.einsum('...j,...jk->...k', row, tm))

    tinv = lax.fori_loop(1, CHUNK, fwd_sub, a) + jnp.eye(CHUNK, dtype=F32)
    u = jnp.einsum('bhnck,bhnkd->bhncd', tinv, vb)
    w = jnp.einsum('bhnck,bhnkd->bhncd', tinv, kb * jnp.exp(gc)[..., None])
    qk = jnp.einsum('bhncd,bhnkd->bhnck', q, k) * decay
    q_dec = q * jnp.exp(gc)[..., None]
    k_dec = k * jnp.exp(gc[..., -1:] - gc)[..., None]
    chunk_decay = jnp.exp(gc[..., -1])
    xs = tuple(jnp.moveaxis(t_, 2, 0) for t_ in (u, w, qk, q_dec, k_dec, chunk_decay))

    def step(state, xs_i):
        u_i, w_i, qk_i, qd_i, kd_i, cd_i = xs_i
        v_new = u_i - jnp.einsum('bhcd,bhde->bhce', w_i, state)
        o = (jnp.einsum('bhcd,bhde->bhce', qd_i, state)
             + jnp.einsum('bhck,bhke->bhce', qk_i, v_new))
        state = state * cd_i[..., None, None] + jnp.einsum('bhcd,bhce->bhde', kd_i, v_new)
        return state, o

    s0 = jnp.zeros((bsz, nh, dk, dv), F32)
    _, o = lax.scan(step, s0, xs)
    return jnp.transpose(o, (1, 0, 3, 2, 4)).reshape(bsz, seq, nh, dv)

def windowed_gqa_with_sink(q, k, v, sink):
    bsz, seq, hq, d = q.shape
    hkv = k.shape[2]
    grp = hq // hkv
    nb = seq // WINDOW
    qb = q.reshape(bsz, nb, WINDOW, hkv, grp, d)

    def band(t):
        tp = jnp.pad(t, ((0, 0), (WINDOW, WINDOW), (0, 0), (0, 0)))
        tp = tp.reshape(bsz, nb + 2, WINDOW, hkv, d)
        return jnp.concatenate([tp[:, :-2], tp[:, 1:-1], tp[:, 2:]], axis=2)

    kw, vw = band(k), band(v)
    s = jnp.einsum('bnqhgd,bnkhd->bnhgqk', qb, kw).astype(F32) * (d ** -0.5)
    i = jnp.arange(WINDOW)
    j = jnp.arange(3 * WINDOW)
    blk = jnp.arange(nb)
    rel = j[None, :] - WINDOW - i[:, None]
    kpos = blk[:, None] * WINDOW - WINDOW + j[None, :]
    mask = (jnp.abs(rel) <= WINDOW)[None] & ((kpos >= 0) & (kpos < seq))[:, None, :]
    mask = mask[None, :, None, None]
    s = jnp.where(mask, s, -jnp.inf)
    sink_l = sink.astype(F32).reshape(1, 1, hkv, grp, 1, 1)
    m = jnp.maximum(jnp.max(s, axis=-1, keepdims=True), sink_l)
    p = jnp.exp(s - m)
    p = p / (jnp.sum(p, axis=-1, keepdims=True) + jnp.exp(sink_l - m))
    o = jnp.einsum('bnhgqk,bnkhd->bnqhgd', p.astype(v.dtype), vw)
    return o.reshape(bsz, seq, hq, d)

def memory_cross_attention(q, k, v):
    d = q.shape[-1]
    s = jnp.einsum('bshd,bmhd->bhsm', q, k).astype(F32) * (d ** -0.5)
    p = jax.nn.softmax(s, axis=-1)
    return jnp.einsum('bhsm,bmhd->bshd', p.astype(v.dtype), v)

def hybrid_layer(h, mem, norm_w, w_in, conv_w_a, a_log_fwd, a_log_bwd, dt_bias_fwd,
                 dt_bias_bwd, o_norm_a, q_norm_b, k_norm_b, sink_b, mem_norm_w, w_mem_kv,
                 q_norm_c, k_norm_c, w_out):
    bsz, seq, _ = h.shape
    hn = rms_norm(h, norm_w)
    proj = hn @ w_in.astype(hn.dtype)
    (qa, ka, va, za, alpha_f, alpha_b, beta_f, beta_b,
     qb, kb, vb, zb, qc, zc) = jnp.split(proj, np.cumsum(IN_SIZES)[:-1].tolist(), axis=-1)

    qkv = jax.nn.silu(centred_depthwise_conv(jnp.concatenate([qa, ka, va], axis=-1), conv_w_a))
    qa, ka, va = jnp.split(qkv, 3, axis=-1)
    qa = l2_norm(qa.reshape(bsz, seq, A_HEADS, A_HEAD_DIM))
    ka = l2_norm(ka.reshape(bsz, seq, A_HEADS, A_HEAD_DIM))
    va = va.reshape(bsz, seq, A_HEADS, A_HEAD_DIM).astype(F32)
    g_f = -jnp.exp(a_log_fwd.astype(F32)) * jax.nn.softplus(alpha_f.astype(F32) + dt_bias_fwd.astype(F32))
    g_b = -jnp.exp(a_log_bwd.astype(F32)) * jax.nn.softplus(alpha_b.astype(F32) + dt_bias_bwd.astype(F32))
    bt_f = jax.nn.sigmoid(beta_f.astype(F32))
    bt_b = jax.nn.sigmoid(beta_b.astype(F32))
    flip = lambda t: jnp.flip(t, axis=1)
    o_fwd = gated_delta_rule_chunked(qa, ka, va, g_f, bt_f)
    o_bwd = flip(gated_delta_rule_chunked(flip(qa), flip(ka), flip(va), flip(g_b), flip(bt_b)))
    o_a = rms_norm((o_fwd + o_bwd).astype(h.dtype), o_norm_a).reshape(bsz, seq, A_WIDTH)
    o_a = o_a * jax.nn.silu(za)

    qb = rope(rms_norm(qb.reshape(bsz, seq, B_Q_HEADS, B_HEAD_DIM), q_norm_b))
    kb = rope(rms_norm(kb.reshape(bsz, seq, B_KV_HEADS, B_HEAD_DIM), k_norm_b))
    vb = vb.reshape(bsz, seq, B_KV_HEADS, B_HEAD_DIM)
    o_b = windowed_gqa_with_sink(qb, kb, vb, sink_b).reshape(bsz, seq, B_WIDTH)
    o_b = o_b * jax.nn.silu(zb)

    mn = rms_norm(mem, mem_norm_w)
    kv_m = mn @ w_mem_kv.astype(mn.dtype)
    km, vm = jnp.split(kv_m, 2, axis=-1)
    mlen = mem.shape[1]
    km = rms_norm(km.reshape(bsz, mlen, C_HEADS, C_HEAD_DIM), k_norm_c)
    vm = vm.reshape(bsz, mlen, C_HEADS, C_HEAD_DIM)
    qc = rms_norm(qc.reshape(bsz, seq, C_HEADS, C_HEAD_DIM), q_norm_c)
    o_c = memory_cross_attention(qc, km, vm).reshape(bsz, seq, C_WIDTH)
    o_c = o_c * jax.nn.silu(zc)

    mixed = jnp.concatenate([o_a.astype(h.dtype), o_b.astype(h.dtype), o_c.astype(h.dtype)], axis=-1)
    return h + mixed @ w_out.astype(h.dtype)

def setup_inputs(seed: int = 0) -> dict:
    key = jax.random.key(seed)
    ks = jax.random.split(key, 20)
    nrm = lambda k_, shape: jax.random.normal(k_, shape, F32)
    x = nrm(ks[0], (BATCH, SEQ, D_MODEL))
    mem = nrm(ks[1], (BATCH, MEM_LEN, D_MODEL))
    norm_w = 1.0 + 0.02 * nrm(ks[2], (DEPTH, D_MODEL))
    w_in = nrm(ks[3], (DEPTH, D_MODEL, IN_WIDTH)) * D_MODEL ** -0.5
    conv_w_a = nrm(ks[4], (DEPTH, CONV_K, 3 * A_WIDTH)) * CONV_K ** -0.5
    a_log_fwd = jnp.log(jax.random.uniform(ks[5], (DEPTH, A_HEADS), F32, 1.0, 16.0))
    a_log_bwd = jnp.log(jax.random.uniform(ks[6], (DEPTH, A_HEADS), F32, 1.0, 16.0))
    dt_f = jnp.exp(jax.random.uniform(ks[7], (DEPTH, A_HEADS), F32, jnp.log(1e-3), jnp.log(1e-1)))
    dt_b = jnp.exp(jax.random.uniform(ks[8], (DEPTH, A_HEADS), F32, jnp.log(1e-3), jnp.log(1e-1)))
    dt_bias_fwd = dt_f + jnp.log(-jnp.expm1(-dt_f))
    dt_bias_bwd = dt_b + jnp.log(-jnp.expm1(-dt_b))
    o_norm_a = 1.0 + 0.02 * nrm(ks[9], (DEPTH, A_HEAD_DIM))
    q_norm_b = 1.0 + 0.02 * nrm(ks[10], (DEPTH, B_HEAD_DIM))
    k_norm_b = 1.0 + 0.02 * nrm(ks[11], (DEPTH, B_HEAD_DIM))
    sink_b = 0.5 * nrm(ks[12], (DEPTH, B_Q_HEADS))
    mem_norm_w = 1.0 + 0.02 * nrm(ks[13], (DEPTH, D_MODEL))
    w_mem_kv = nrm(ks[14], (DEPTH, D_MODEL, 2 * C_WIDTH)) * D_MODEL ** -0.5
    q_norm_c = 1.0 + 0.02 * nrm(ks[15], (DEPTH, C_HEAD_DIM))
    k_norm_c = 1.0 + 0.02 * nrm(ks[16], (DEPTH, C_HEAD_DIM))
    w_out = nrm(ks[17], (DEPTH, MIX_WIDTH, D_MODEL)) * MIX_WIDTH ** -0.5
    return {"x": x, "mem": mem, "norm_w": norm_w, "w_in": w_in, "conv_w_a": conv_w_a,
            "a_log_fwd": a_log_fwd, "a_log_bwd": a_log_bwd, "dt_bias_fwd": dt_bias_fwd,
            "dt_bias_bwd": dt_bias_bwd, "o_norm_a": o_norm_a, "q_norm_b": q_norm_b,
            "k_norm_b": k_norm_b, "sink_b": sink_b, "mem_norm_w": mem_norm_w,
            "w_mem_kv": w_mem_kv, "q_norm_c": q_norm_c, "k_norm_c": k_norm_c, "w_out": w_out}

def reference(x, mem, norm_w, w_in, conv_w_a, a_log_fwd, a_log_bwd, dt_bias_fwd, dt_bias_bwd,
              o_norm_a, q_norm_b, k_norm_b, sink_b, mem_norm_w, w_mem_kv, q_norm_c, k_norm_c,
              w_out):
    h = x
    for l in range(DEPTH):
        h = hybrid_layer(h, mem, norm_w[l], w_in[l], conv_w_a[l], a_log_fwd[l], a_log_bwd[l],
                         dt_bias_fwd[l], dt_bias_bwd[l], o_norm_a[l], q_norm_b[l], k_norm_b[l],
                         sink_b[l], mem_norm_w[l], w_mem_kv[l], q_norm_c[l], k_norm_c[l], w_out[l])
    return h


_drawn_inputs = setup_inputs


def setup_inputs(seed=0):
    import zlib

    import numpy as np

    out = dict(_drawn_inputs(seed))
    spreads = {}
    factors = {'norm_w': 4.548,
     'o_norm_a': 22.56,
     'q_norm_b': 22.415,
     'k_norm_b': 23.25,
     'sink_b': 8.0,
     'mem_norm_w': 8.0,
     'q_norm_c': 8.0,
     'k_norm_c': 8.0}
    for name, (base, spread) in spreads.items():
        noise = np.random.default_rng([zlib.crc32(name.encode()), seed]).standard_normal(out[name].shape)
        drawn = base * np.exp(spread * noise) if base else spread * noise
        out[name] = __import__('jax').numpy.asarray(drawn.astype(out[name].dtype))
    for name, factor in factors.items():
        out[name] = (out[name] * factor).astype(out[name].dtype)
    return out
```

```python
from contextlib import ExitStack

import numpy as np
import concourse.bass as bass
from concourse import mybir

ALU = mybir.AluOpType
ACT = mybir.ActivationFunctionType
AX_X = mybir.AxisListType.X
F32 = mybir.dt.float32
F32R = mybir.dt.float32r

P = 128
D_MODEL, SEQ, MEM_LEN = 2048, 1024, 256
KT = D_MODEL // P
HALF = 512
NH = SEQ // HALF
A_HEADS, CONV_K, PAD = 8, 5, 2
CHUNK = 128
NC = SEQ // CHUNK
B_HEADS, B_DIM, WINDOW = 8, 64, 128
C_HEADS = 4
EPS = 1e-6
NEG = -1e30

T_A = 0
T_BQ = 4 * A_HEADS
T_BK = T_BQ + 4
T_BV = T_BK + 1
T_BZ = T_BV + 1
T_CZ = T_BZ + 4
T_CQ = T_CZ + 4
T_GATE = T_CQ + 4
TILES = T_GATE + 1
LEVELS = (2, 4, 8, 16, 32, 64)


class Names:

    def __init__(self, nc, stack, prefix):
        self.nc, self.stack, self.prefix = nc, stack, prefix
        self.sems = []

    def sb(self, name, shape, dt=F32):
        return self.stack.enter_context(self.nc.sbuf_tensor(self.prefix + name, shape, dt))

    def ps(self, name, shape, dt=F32):
        return self.stack.enter_context(self.nc.psum_tensor(self.prefix + name, shape, dt))

    def sem(self, name):
        self.sems.append(self.nc.alloc_semaphore(name=self.prefix + name))
        return self.sems[-1]


def split_product(pe, out, w_hi, w_lo, x_hi, x_lo, first, last):
    pe.matmul(out, w_lo, x_hi, start=first, stop=False)
    pe.matmul(out, w_hi, x_lo, start=False, stop=False)
    return pe.matmul(out, w_hi, x_hi, start=False, stop=last)


def memory_stage(nc, c, mem_t, mem_norm_w, w_mem, k_norm_c, kv_scratch):
    MT, WQ = MEM_LEN // P, 4
    with ExitStack() as stack:
        n = Names(nc, stack, "mem_")
        raw, nw = n.sb("raw", [P, KT, MEM_LEN]), n.sb("nw", [P, KT])
        sq, normed = n.sb("sq", [P, KT, MEM_LEN]), n.sb("normed", [P, KT, MEM_LEN])
        hi, lo = n.sb("hi", [P, KT, MEM_LEN], F32R), n.sb("lo", [P, KT, MEM_LEN], F32R)
        w_raw = n.sb("w_raw", [P, 2, 4, 2 * HALF])
        w_hi, w_lo = n.sb("w_hi", [P, 2, 4, 2 * HALF], F32R), n.sb("w_lo", [P, 2, 4, 2 * HALF], F32R)
        rstd = n.sb("rstd", [P, MEM_LEN])
        kv, ksq = n.sb("kv", [P, MT, 2, HALF]), n.sb("ksq", [P, MT, HALF])
        kss, kn = n.sb("kss", [P, MT, C_HEADS]), n.sb("kn", [P, P])
        ps_sum, ps_kv = n.ps("ps_sum", [P, HALF]), n.ps("ps_kv", [P, MT, 2, HALF])
        s_in, s_kn = n.sem("s_in"), n.sem("s_kn")
        s_w = [n.sem(f"s_w{i}") for i in range(2)]
        s_sq, s_sum, s_root, s_rstd, s_norm = (n.sem(x) for x in ("s_sq", "s_sum", "s_root", "s_rstd", "s_norm"))
        s_hi, s_lo, s_whi, s_wlo, s_used = (n.sem(x) for x in ("s_hi", "s_lo", "s_whi", "s_wlo", "s_used"))
        s_kv, s_out, s_ksq, s_kss, s_kr, s_kd, s_st = (
            n.sem(x) for x in ("s_kv", "s_out", "s_ksq", "s_kss", "s_kr", "s_kd", "s_st"))
        block = stack.enter_context(nc.Block())

        @block.sync
        def _(sp):
            sp.dma_start(raw[:], mem_t).then_inc(s_in, 16)
            sp.dma_start(nw[:], mem_norm_w).then_inc(s_in, 16)
            sp.dma_start(kn[:], k_norm_c.rearrange("(a n) -> a n", a=1).partition_broadcast(P)).then_inc(s_kn, 16)
            for q in range(WQ):
                if q >= 2:
                    sp.wait_ge(s_whi, q - 1)
                    sp.wait_ge(s_wlo, q - 1)
                sp.dma_start(w_raw[:, q % 2], w_mem[:, 4 * q:4 * q + 4]).then_inc(s_w[q % 2], 16)
            sp.wait_ge(s_kd, 2 * MT)
            sp.wait_ge(s_out, 2 * MT)
            sp.dma_start(kv_scratch, kv[:]).then_inc(s_st, 16)
            sp.wait_ge(s_st, 16)

        @block.scalar
        def _(act):
            act.wait_ge(s_in, 32)
            act.activation(sq[:], raw[:], ACT.Square).then_inc(s_sq, 1)
            act.wait_ge(s_sum, 1)
            act.activation(rstd[:], ps_sum[:, 0:MEM_LEN], ACT.Sqrt, scale=1.0 / D_MODEL,
                           bias=c["eps"][:, 0:1]).then_inc(s_root, 1)
            act.wait_ge(s_norm, 1)
            act.activation(hi[:], normed[:], ACT.Copy).then_inc(s_hi, 1)
            for q in range(WQ):
                act.wait_ge(s_w[q % 2], 16 * (q // 2 + 1))
                if q >= 2:
                    act.wait_ge(s_used, q - 1)
                act.activation(w_hi[:, q % 2], w_raw[:, q % 2], ACT.Copy).then_inc(s_whi, 1)
            act.wait_ge(s_kv, 1)
            for m in range(MT):
                for j in range(2):
                    act.activation(kv[:, m, j], ps_kv[:, m, j], ACT.Copy).then_inc(s_out, 1)
            act.wait_ge(s_out, 2 * MT)
            for m in range(MT):
                act.activation(ksq[:, m], kv[:, m, 0], ACT.Square).then_inc(s_ksq, 1)
            act.wait_ge(s_kss, 1)
            act.activation(kss[:], kss[:], ACT.Sqrt, scale=1.0 / P, bias=c["eps"][:, 0:1]).then_inc(s_kr, 1)

        @block.vector
        def _(dve):
            dve.wait_ge(s_root, 1)
            dve.reciprocal(rstd[:], rstd[:]).then_inc(s_rstd, 1)
            dve.wait_ge(s_rstd, 1)
            for k in range(KT):
                last = dve.scalar_tensor_tensor(normed[:, k], raw[:, k], nw[:, k:k + 1], rstd[:],
                                                ALU.mult, ALU.mult)
            last.then_inc(s_norm, 1)
            dve.wait_ge(s_hi, 1)
            dve.tensor_tensor(lo[:], normed[:], hi[:].bitcast(F32), ALU.subtract).then_inc(s_lo, 1)
            for q in range(WQ):
                dve.wait_ge(s_whi, q + 1)
                if q >= 2:
                    dve.wait_ge(s_used, q - 1)
                dve.tensor_tensor(w_lo[:, q % 2], w_raw[:, q % 2], w_hi[:, q % 2].bitcast(F32),
                                  ALU.subtract).then_inc(s_wlo, 1)
            dve.wait_ge(s_ksq, MT)
            dve.tensor_reduce(kss[:], ksq[:].rearrange("p m (h d) -> p m h d", h=C_HEADS),
                              AX_X, ALU.add).then_inc(s_kss, 1)
            dve.wait_ge(s_kr, 1)
            dve.reciprocal(kss[:], kss[:]).then_inc(s_kss, 1)
            dve.wait_ge(s_kss, 2)
            dve.wait_ge(s_kn, 16)
            for m in range(MT):
                keys = kv[:, m, 0].rearrange("p (h d) -> p h d", h=C_HEADS)
                dve.tensor_tensor(keys, keys, kss[:, m, :, None].to_broadcast([P, C_HEADS, P]),
                                  ALU.mult).then_inc(s_kd, 1)
                dve.wait_ge(s_kd, 2 * m + 1)
                dve.tensor_tensor(keys, keys, kn[:, None, :].to_broadcast([P, C_HEADS, P]),
                                  ALU.mult).then_inc(s_kd, 1)

        @block.tensor
        def _(pe):
            pe.wait_ge(s_sq, 1)
            for k in range(KT):
                last = pe.matmul(ps_sum[:, 0:MEM_LEN], c["ones"][:], sq[:, k], start=k == 0, stop=k == KT - 1)
            last.then_inc(s_sum, 1)
            pe.wait_ge(s_hi, 1)
            pe.wait_ge(s_lo, 1)
            for q in range(WQ):
                pe.wait_ge(s_whi, q + 1)
                pe.wait_ge(s_wlo, q + 1)
                for k in range(4 * q, 4 * q + 4):
                    for m in range(MT):
                        rows = slice(m * P, (m + 1) * P)
                        for j in range(2):
                            cols = slice(j * HALF, (j + 1) * HALF)
                            last = split_product(pe, ps_kv[:, m, j], hi[:, k, rows], lo[:, k, rows],
                                                 w_hi[:, q % 2, k % 4, cols], w_lo[:, q % 2, k % 4, cols],
                                                 k == 0, k == KT - 1)
                last.then_inc(s_used, 1)
            pe.matmul(ps_sum[:, 0:1], c["ones"][:], c["ones"][:, 0:1], start=True, stop=True).then_inc(s_kv, 1)
    nc.clear_and_free_semaphores(n.sems)
    nc.all_engine_barrier()


def input_norm_stage(nc, c, x_t, norm_w, x_hi, x_lo):
    LOADS = 4
    PER = KT // LOADS
    with ExitStack() as stack:
        n = Names(nc, stack, "xn_")
        raw, nw = n.sb("raw", [P, KT, SEQ]), n.sb("nw", [P, KT])
        tmp = n.sb("tmp", [P, 2, SEQ // 2])
        rstd = n.sb("rstd", [P, SEQ])
        ps_sum = n.ps("ps_sum", [P, SEQ])
        s_in = [n.sem(f"s_in{i}") for i in range(LOADS)]
        s_nw = n.sem("s_nw")
        s_sq, s_sum, s_root, s_rstd, s_norm, s_hi, s_lo = (
            n.sem(x) for x in ("s_sq", "s_sum", "s_root", "s_rstd", "s_norm", "s_hi", "s_lo"))
        block = stack.enter_context(nc.Block())
        pieces = [(k, h) for k in range(KT) for h in range(NH)]

        @block.sync
        def _(sp):
            for i in range(LOADS):
                sp.dma_start(raw[:, PER * i:PER * i + PER], x_t[:, PER * i:PER * i + PER]).then_inc(s_in[i], 16)
            sp.dma_start(nw[:], norm_w).then_inc(s_nw, 16)

        @block.scalar
        def _(act):
            for i, (k, h) in enumerate(pieces):
                act.wait_ge(s_in[k // PER], 16)
                if i >= 2:
                    act.wait_ge(s_sum, i - 1)
                act.activation(tmp[:, i % 2], raw[:, k, bass.ts(h, HALF)], ACT.Square).then_inc(s_sq, 1)
            act.wait_ge(s_sum, len(pieces))
            act.activation(rstd[:], ps_sum[:], ACT.Sqrt, scale=1.0 / D_MODEL,
                           bias=c["eps"][:, 0:1]).then_inc(s_root, 1)
            for k in range(KT):
                act.wait_ge(s_norm, k + 1)
                act.activation(x_hi[:, k], raw[:, k], ACT.Copy).then_inc(s_hi, 1)

        @block.tensor
        def _(pe):
            for i, (k, h) in enumerate(pieces):
                pe.wait_ge(s_sq, i + 1)
                pe.matmul(ps_sum[:, bass.ts(h, HALF)], c["ones"][:], tmp[:, i % 2], start=k == 0,
                          stop=k == KT - 1).then_inc(s_sum, 1)

        @block.vector
        def _(dve):
            dve.wait_ge(s_root, 1)
            dve.reciprocal(rstd[:], rstd[:]).then_inc(s_rstd, 1)
            dve.wait_ge(s_rstd, 1)
            dve.wait_ge(s_nw, 16)

            def norm(k):
                dve.scalar_tensor_tensor(raw[:, k], raw[:, k], nw[:, k:k + 1], rstd[:],
                                         ALU.mult, ALU.mult).then_inc(s_norm, 1)

            norm(0)
            for k in range(KT):
                if k + 1 < KT:
                    norm(k + 1)
                dve.wait_ge(s_hi, k + 1)
                dve.tensor_tensor(x_lo[:, k], raw[:, k], x_hi[:, k].bitcast(F32), ALU.subtract).then_inc(s_lo, 1)


def projection_stage(nc, c, w_in, conv_w, x_hi, x_lo, proj):
    UNIT = KT // 2
    STEPS = T_GATE // 2
    SEGMENTS = ((T_A, 4, A_HEADS, "cccz"), (T_BQ, 2, 3, "pp"), (T_BZ, 2, 4, "zz"), (T_CQ, 2, 2, "pp"),
                (T_GATE, 1, 1, "p"))
    with ExitStack() as stack:
        n = Names(nc, stack, "pr_")
        w_raw = n.sb("w_raw", [P, 4, UNIT * P])
        w_hi, w_lo = n.sb("w_hi", [P, 4, UNIT * P], F32R), n.sb("w_lo", [P, 4, UNIT * P], F32R)
        padded = n.sb("padded", [P, 2, SEQ + 2 * PAD])
        conv, th, res = n.sb("conv", [P, SEQ]), n.sb("th", [P, SEQ]), n.sb("res", [P, 2, SEQ])
        taps, head_taps = n.sb("taps", [P, 3 * A_HEADS * CONV_K]), n.sb("head_taps", [P, 3 * CONV_K])
        acc = n.ps("acc", [P, 4, HALF])
        s_raw = [n.sem(f"s_raw{i}") for i in range(4)]
        s_hi, s_lo, s_acc, s_taps, s_head_taps, s_margin = (
            n.sem(x) for x in ("s_hi", "s_lo", "s_acc", "s_taps", "s_head_taps", "s_margin"))
        s_taken, s_tap, s_th, s_res = (n.sem(x) for x in ("s_taken", "s_tap", "s_th", "s_res"))
        s_st, s_left = n.sem("s_st"), n.sem("s_left")
        block = stack.enter_context(nc.Block())
        TAKEN0, RES0, LEFT0 = 4, 2, 2

        def each_step(eng, body):
            convs = ths = 0
            for first, width, steps, kinds in SEGMENTS:
                nc_, nt = kinds.count("c"), width - kinds.count("p")
                if steps > 2:
                    with eng.Fori(0, steps) as i:
                        body(i, i * width + first, i * (width // 2) + first // 2, kinds, i * nc_ + convs, i * nt + ths)
                else:
                    for i in range(steps):
                        body(i, i * width + first, i * (width // 2) + first // 2, kinds, i * nc_ + convs, i * nt + ths)
                convs, ths = convs + steps * nc_, ths + steps * nt

        def has_next(t):
            return not isinstance(t, int) or t + 2 < TILES

        @block.sync
        def _(sp):
            def load(t, b):
                sp.dma_start(w_raw[:, b], w_in[bass.ds(t, 1), :, bass.ts(b % 2, UNIT * P)]
                             .rearrange("a p n -> p (a n)")).then_inc(s_raw[b], 16)

            for b in range(4):
                load(b // 2, b)
            with sp.Fori(1, STEPS) as i:
                for b in range(4):
                    sp.wait_ge(s_lo, i * 4 + (b - 3))
                    load(i * 2 + b // 2, b)
            for b in range(2):
                sp.wait_ge(s_lo, STEPS * 4 + b - 3)
                load(T_GATE, b)

        @block.gpsimd
        def _(pool):
            pool.sem_inc(s_left, LEFT0)
            pool.dma_start(taps[:], conv_w).then_inc(s_taps, 16)
            for j in range(2):
                pool.memset(padded[:, j, 0:PAD], 0.0).then_inc(s_margin, 1)
                pool.memset(padded[:, j, PAD + SEQ:], 0.0).then_inc(s_margin, 1)

            def store(i, first, pair, kinds, convs, ths):
                for j in range(len(kinds)):
                    pool.wait_ge(s_res, first + (j + 1 + RES0))
                    pool.dma_start(proj[bass.ds(first + j, 1)].rearrange("a p n -> p (a n)"),
                                   res[:, j % 2]).then_inc(s_st, 16)
                    pool.wait_ge(s_st, first * 16 + 16 * (j + 1))
                    pool.sem_inc(s_left, 1)

            each_step(pool, store)

        @block.tensor
        def _(pe):
            def tile(parity, t):
                for u in range(2):
                    b = 2 * parity + u
                    pe.wait_ge(s_hi, t * 2 + (u + 1))
                    pe.wait_ge(s_lo, t * 2 + (u + 1))
                    if u == 0:
                        pe.wait_ge(s_taken, t * 2 + (TAKEN0 - 2))
                    for h in range(NH):
                        for k in range(UNIT):
                            last = split_product(
                                pe, acc[:, 2 * parity + h], w_hi[:, b, bass.ts(k, P)], w_lo[:, b, bass.ts(k, P)],
                                x_hi[:, u * UNIT + k, bass.ts(h, HALF)], x_lo[:, u * UNIT + k, bass.ts(h, HALF)],
                                u == 0 and k == 0, u == 1 and k == UNIT - 1)
                        if u == 1:
                            last.then_inc(s_acc, 1)

            with pe.Fori(0, STEPS) as i:
                tile(0, i * 2)
                tile(1, i * 2 + 1)
            tile(0, T_GATE)

        @block.scalar
        def _(act):
            def high_part(b):
                act.activation(w_hi[:, b], w_raw[:, b], ACT.Copy).then_inc(s_hi, 1)

            act.sem_inc(s_taken, TAKEN0)
            for b in range(4):
                act.wait_ge(s_raw[b], 16)
                high_part(b)

            def step(i, first, pair, kinds, convs, ths):
                for j, kind in enumerate(kinds):
                    t, parity = first + j, j % 2
                    act.wait_ge(s_res, t + (RES0 - 1))
                    for h in range(NH):
                        act.wait_ge(s_acc, t * 2 + (h + 1))
                        act.activation(padded[:, parity, PAD + h * HALF:PAD + (h + 1) * HALF],
                                       acc[:, 2 * parity + h], ACT.Copy).then_inc(s_taken, 1)
                    if has_next(t):
                        for b in (2 * parity, 2 * parity + 1):
                            act.wait_ge(s_raw[b], pair * 16 + (16 * (j // 2 + 2)))
                            high_part(b)
                    if kind != "p":
                        act.wait_ge(s_res, t + RES0)
                    if kind == "c":
                        act.wait_ge(s_tap, (convs + kinds[:j].count("c")) * CONV_K + CONV_K)
                        act.activation(th[:], conv[:], ACT.Tanh, scale=0.5).then_inc(s_th, 1)
                    elif kind == "z":
                        act.wait_ge(s_taken, t * 2 + (TAKEN0 + 2))
                        act.activation(th[:], padded[:, parity, PAD:PAD + SEQ], ACT.Tanh, scale=0.5).then_inc(s_th, 1)

            each_step(act, step)

        @block.vector
        def _(dve):
            dve.sem_inc(s_res, RES0)
            for b in range(4):
                dve.wait_ge(s_hi, b + 1)
                dve.tensor_tensor(w_lo[:, b], w_raw[:, b], w_hi[:, b].bitcast(F32), ALU.subtract).then_inc(s_lo, 1)
            dve.wait_ge(s_taps, 16)
            dve.wait_ge(s_margin, 4)

            def step(i, first, pair, kinds, convs, ths):
                if "c" in kinds:
                    dve.tensor_copy(head_taps[:], taps[:, bass.ds(i * (3 * CONV_K), 3 * CONV_K)]).then_inc(s_head_taps, 1)
                    dve.wait_ge(s_head_taps, i + 1)
                for j, kind in enumerate(kinds):
                    t, parity = first + j, j % 2
                    body = padded[:, parity, PAD:PAD + SEQ]
                    dve.wait_ge(s_taken, t * 2 + (TAKEN0 + 2))
                    if kind == "c":
                        done = (convs + kinds[:j].count("c")) * CONV_K
                        dve.wait_ge(s_res, t + RES0)
                        for tap in range(CONV_K):
                            src, w = padded[:, parity, tap:tap + SEQ], head_taps[:, j * CONV_K + tap:j * CONV_K + tap + 1]
                            if tap == 0:
                                dve.tensor_scalar(conv[:], src, w, None, ALU.mult).then_inc(s_tap, 1)
                            else:
                                dve.wait_ge(s_tap, done + tap)
                                dve.scalar_tensor_tensor(conv[:], src, w, conv[:], ALU.mult, ALU.add).then_inc(s_tap, 1)
                        body = conv[:]
                    if has_next(t):
                        for u in range(2):
                            b = 2 * parity + u
                            dve.wait_ge(s_hi, t * 2 + (4 + u + 1))
                            dve.tensor_tensor(w_lo[:, b], w_raw[:, b], w_hi[:, b].bitcast(F32),
                                              ALU.subtract).then_inc(s_lo, 1)
                    dve.wait_ge(s_left, t + (LEFT0 - 1))
                    if kind == "p":
                        dve.tensor_copy(res[:, parity], body).then_inc(s_res, 1)
                    else:
                        dve.wait_ge(s_th, ths + (j + 1 - kinds[:j].count("p")))
                        dve.scalar_tensor_tensor(res[:, parity], th[:], 1.0, body, ALU.add, ALU.mult).then_inc(s_res, 1)

            each_step(dve, step)

def gate_stage(nc, c, proj, gate_consts, gate_rows, cols):
    with ExitStack() as stack:
        n = Names(nc, stack, "gt_")
        raw, g, rows, resets = n.sb("raw", [P, SEQ]), n.sb("g", [P, SEQ]), n.sb("rows", [P, SEQ]), n.sb("resets", [P, SEQ])
        pos, small = n.sb("pos", [P, SEQ]), n.sb("small", [P, 4])
        ps = n.ps("ps", [P, 2, HALF])
        s_in, s_g, s_a, s_rows, s_tr, s_st, s_cols = (
            n.sem(x) for x in ("s_in", "s_g", "s_a", "s_rows", "s_tr", "s_st", "s_cols"))
        s_resets = n.sem("s_resets")
        block = stack.enter_context(nc.Block())
        LOW, HIGH = slice(0, P // 2), slice(P // 2, P)

        @block.sync
        def _(sp):
            sp.dma_start(raw[:], proj[T_GATE]).then_inc(s_in, 16)
            sp.dma_start(small[:, 0:2], gate_consts).then_inc(s_in, 16)
            sp.wait_ge(s_rows, 4)
            for group in range(4):
                sp.dma_start(gate_rows[group], rows[32 * group:32 * group + A_HEADS, :]).then_inc(s_st, 16)
            sp.wait_ge(s_st, 64)

        @block.gpsimd
        def _(pool):
            pool.memset(resets[:], 1.0).then_inc(s_resets, 1)
            pool.wait_ge(s_resets, 1)
            pool.memset(resets[:].rearrange("p (n i) -> p n i", i=CHUNK)[:, :, 0:1], 0.0).then_inc(s_resets, 1)

        @block.scalar
        def _(act):
            act.wait_ge(s_in, 32)
            act.activation(small[:, 2:3], small[:, 1:2], ACT.Exp).then_inc(s_a, 1)
            act.activation(g[HIGH, :], raw[HIGH, :], ACT.Exp, scale=-1.0).then_inc(s_a, 1)
            act.wait_ge(s_g, 1)
            act.activation(g[LOW, :], raw[LOW, :], ACT.Abs).then_inc(s_a, 1)
            act.wait_ge(s_a, 3)
            act.activation(g[LOW, :], g[LOW, :], ACT.Exp, scale=-1.0).then_inc(s_a, 1)
            act.wait_ge(s_a, 4)
            act.activation(g[LOW, :], g[LOW, :], ACT.Ln, bias=c["one"][LOW, 0:1]).then_inc(s_a, 1)

        @block.vector
        def _(dve):
            dve.wait_ge(s_in, 32)
            dve.tensor_scalar(raw[LOW, :], raw[LOW, :], small[LOW, 0:1], None, ALU.add).then_inc(s_g, 1)
            dve.wait_ge(s_g, 1)
            dve.tensor_scalar(pos[LOW, :], raw[LOW, :], 0.0, None, ALU.max).then_inc(s_g, 1)
            dve.wait_ge(s_a, 5)
            dve.wait_ge(s_g, 2)
            dve.tensor_tensor(pos[LOW, :], pos[LOW, :], g[LOW, :], ALU.add).then_inc(s_g, 1)
            dve.wait_ge(s_g, 3)
            dve.tensor_scalar(pos[LOW, :], pos[LOW, :], small[LOW, 2:3], -1.0, ALU.mult, ALU.mult).then_inc(s_g, 1)
            dve.tensor_scalar(g[HIGH, :], g[HIGH, :], 1.0, None, ALU.add).then_inc(s_g, 1)
            dve.wait_ge(s_g, 5)
            dve.wait_ge(s_resets, 2)
            dve.tensor_tensor_scan(rows[0:32, :], resets[0:32, :], pos[0:32, :], 0.0, ALU.mult, ALU.add).then_inc(s_rows, 1)
            dve.tensor_tensor_scan(rows[32:64, ::-1], resets[32:64, :], pos[32:64, ::-1], 0.0,
                                   ALU.mult, ALU.add).then_inc(s_rows, 1)
            dve.reciprocal(rows[64:96, :], g[64:96, :]).then_inc(s_rows, 1)
            dve.reciprocal(rows[96:128, :], g[96:128, :]).then_inc(s_rows, 1)
            for half in range(2):
                dve.wait_ge(s_tr, half + 1)
                for group in range(4):
                    src = ps[:, half].rearrange("p (n r) -> p r n", r=P)[:, 32 * group:32 * group + A_HEADS, :]
                    dve.tensor_copy(cols[:, group, :, 4 * half:4 * half + 4], src).then_inc(s_cols, 1)

        @block.tensor
        def _(pe):
            pe.wait_ge(s_rows, 4)
            for half in range(2):
                for n_ in range(4):
                    last = pe.transpose(ps[:, half, bass.ts(n_, P)], rows[:, bass.ts(4 * half + n_, P)], c["ident"][:])
                last.then_inc(s_tr, 1)


def delta_stage(nc, c, proj, gate_rows, cols, o_norm, mixed):
    NT = 2 * NC
    with ExitStack() as stack:
        n = Names(nc, stack, "dl_")
        qk, v, z = n.sb("qk", [P, 2, SEQ]), n.sb("v", [P, SEQ]), n.sb("z", [P, 2, SEQ])
        grow, brow = n.sb("grow", [P, 2, SEQ]), n.sb("brow", [P, 2, SEQ])
        dec, root = n.sb("dec", [P, NT, P]), n.sb("root", [P, 2, SEQ])
        k_rows, v_rows = n.sb("k_rows", [P, NC, P]), n.sb("v_rows", [P, NC, P])
        hc = n.sb("hc", [P, 4, NC])
        negc, egc, kdc, hb, beg = (n.sb(x, [P, 2, NC]) for x in ("negc", "egc", "kdc", "hb", "beg"))
        glast, cdec = n.sb("glast", [P, 2, NC]), n.sb("cdec", [P, 2, 2, NC])
        mt, wt = n.sb("mt", [P, NT, P]), n.sb("wt", [P, NT, P])
        d, zz = wt[:, 0:NC], wt[:, NC:NT]
        dt, pt = n.sb("dt", [P, 2, NT, P]), n.sb("pt", [P, 2, NT, P])
        kd, kbe, vb, qd = (n.sb(x, [P, 2, NT, P]) for x in ("kd", "kbe", "vb", "qd"))
        vnew, state = n.sb("vnew", [P, 2, 2, P]), n.sb("state", [P, 2, 2, P])
        osq, fin = n.sb("osq", [P, SEQ]), n.sb("fin", [P, SEQ])
        onorm = n.sb("onorm", [P, 1])
        ring, pp, po = n.ps("ring", [P, 4, HALF]), n.ps("pp", [P, 2, HALF]), n.ps("po", [P, 2, HALF])
        masks, neg, one_level, ident = c["masks"], c["neg"], c["level1"], c["ident"]

        l_qk, l_v, l_g, l_b, l_z, l_on = (n.sem(x) for x in ("l_qk", "l_v", "l_g", "l_b", "l_z", "l_on"))
        e_sq, e_nm, e_rt, e_rc, e_hat = (n.sem(x) for x in ("e_sq", "e_nm", "e_rt", "e_rc", "e_hat"))
        e_hc, e_ec, e_gl, e_dif, e_col = (n.sem(x) for x in ("e_hc", "e_ec", "e_gl", "e_dif", "e_col"))
        e_neg, e_dec, e_eg, e_kb, e_qd = (n.sem(x) for x in ("e_neg", "e_dec", "e_eg", "e_kb", "e_qd"))
        e_tr, e_rows, e_scaled = (n.sem(x) for x in ("e_tr", "e_rows", "e_scaled"))
        e_qk, e_pt, e_g, e_mt, e_d1 = (n.sem(x) for x in ("e_qk", "e_pt", "e_g", "e_mt", "e_d1"))
        e_both = n.sem("e_both")
        s_t, s_td, s_z, s_zd, s_i, s_id = (n.sem(x) for x in ("s_t", "s_td", "s_z", "s_zd", "s_i", "s_id"))
        s_w, s_wd, s_vn, s_vd, s_s, s_sd, s_o = (
            n.sem(x) for x in ("s_w", "s_wd", "s_vn", "s_vd", "s_s", "s_sd", "s_o"))
        f_sq, f_nm, f_rt, f_rc, f_x, f_res, f_st = (
            n.sem(x) for x in ("f_sq", "f_nm", "f_rt", "f_rc", "f_x", "f_res", "f_st"))
        block = stack.enter_context(nc.Block())
        E0, M0 = 2, 4
        L = len(LEVELS)
        LT, LZ = 4 * L, 4 * L
        KS = 2 * (NC - 1)

        def heads(eng, slot, first=None, last=None):
            slot(0, 0, True, False)
            slot(1, 1, True, True)
            with eng.Fori(1, A_HEADS // 2 - 1) as i:
                slot(i * 2, 0, True, True)
                slot(i * 2 + 1, 1, True, True)
            slot(A_HEADS - 2, 0, True, True)
            slot(A_HEADS - 1, 1, False, True)

        def after_first(h):
            return not isinstance(h, int) or h > 0

        def alternating(tile, other, width, size):
            return bass.AP(tensor=tile.tensor, offset=tile.offset,
                           ap=[list(tile.ap[0]), [2 * size, width // (2 * size)], [size + other, 2], [1, size]])

        def left_d(parity, chunk, count, level):
            return alternating(dt[:, parity, NC + chunk], -NC * P, count * P, LEVELS[level])

        def as_blocks(tile, size):
            return tile.rearrange("p (m e i) -> p m e i", e=2, i=size)

        def chunk_of(direction, t):
            return t if direction == 0 else NC - 1 - t

        @block.sync
        def _(sp):
            sp.dma_start(onorm[:], o_norm).then_inc(l_on, 16)

            def tiles(h, j, k=1):
                return proj[bass.ds(h * 4 + j, k)].rearrange("a p n -> p a n")

            def load(h, parity, again):
                if again:
                    sp.wait_ge(e_tr, h * 4)
                    sp.wait_ge(e_g, h * 4)
                    sp.wait_ge(e_qd, h * 4)
                sp.dma_start(qk[:], tiles(h, 0, 2)).then_inc(l_qk, 16)
                sp.dma_start(grow[:], row_source(0, h)).then_inc(l_g, 16)
                sp.dma_start(brow[:], row_source(2, h)).then_inc(l_b, 16)
                sp.dma_start(v[:], proj[bass.ds(h * 4 + 2, 1)].rearrange("a p n -> p (a n)")).then_inc(l_v, 16)

            def load_z(h, parity, again):
                if again:
                    sp.wait_ge(l_z, h * 16)
                    sp.wait_ge(f_res, h - 1)
                sp.dma_start(z[:, parity], proj[bass.ds(h * 4 + 3, 1)].rearrange("a p n -> p (a n)")).then_inc(l_z, 16)

            def row_source(group, h):
                return gate_rows[group:group + 2, bass.ds(h, 1), :].rearrange("g a n -> (a g) n").partition_broadcast(P)

            load(0, 0, False)
            load_z(0, 0, False)

            def slot(h, parity, more, before):
                if more:
                    load(h + 1, 1 - parity, True)
                    load_z(h + 1, 1 - parity, before)
                if before:
                    store(h - 1)

            def store(h):
                sp.wait_ge(f_res, h + 1)
                sp.dma_start(mixed[bass.ds(h, 1)].rearrange("a p n -> p (a n)"), fin[:]).then_inc(f_st, 16)

            heads(sp, slot)
            store(A_HEADS - 1)
            sp.wait_ge(f_st, 16 * A_HEADS)

        @block.scalar
        def _(act):
            def squares(g):
                act.wait_ge(l_qk, g * 16 + 16)
                act.wait_ge(e_hat, g * 2 + E0)
                for j in (1, 0):
                    act.activation(root[:, j], qk[:, j], ACT.Square).then_inc(e_sq, 1)

            def roots(g, j):
                for half in range(2):
                    act.wait_ge(e_nm, g * 4 + (2 * (1 - j) + half + 1))
                    act.activation(root[:, j, bass.ts(half, HALF)], pp[:, half], ACT.Sqrt,
                                   bias=c["eps4"][:, 0:1]).then_inc(e_rt, 1)

            def column_exps(g, parity):
                act.wait_ge(e_hc, g + 1)
                act.wait_ge(e_dif, g + 1)
                act.activation(egc[:], hc[:, 0:2], ACT.Exp).then_inc(e_ec, 1)
                act.activation(kdc[:], kdc[:], ACT.Exp).then_inc(e_ec, 1)
                act.activation(cdec[:, parity], glast[:], ACT.Exp).then_inc(e_ec, 1)

            def decays(g, first, count):
                for tile in range(first, first + count):
                    direction, chunk = divmod(tile, NC)
                    act.wait_ge(e_neg, g * 2 + (direction + 1))
                    act.wait_ge(e_col, g * 3 + 1)
                    act.activation(dec[:, tile], dec[:, tile], ACT.Exp,
                                   bias=negc[:, direction, chunk:chunk + 1]).then_inc(e_dec, 1)

            def row_exps(g):
                act.wait_ge(e_neg, g * 2 + 2)
                act.wait_ge(e_gl, g * 2 + 2)
                for direction in range(2):
                    act.activation(grow[:, direction], grow[:, direction], ACT.Exp).then_inc(e_eg, 1)

            def row_copies(g, which):
                if after_first(g):
                    act.wait_ge(e_scaled, g * 6)
                for half in range(2):
                    act.wait_ge(e_tr, g * 4 + (2 * which + half + 1))
                    act.activation((k_rows, v_rows)[which][:, 4 * half:4 * half + 4], pp[:, half]
                                   .rearrange("p (a n) -> p a n", n=P), ACT.Copy).then_inc(e_rows, 1)

            def end_squares(f):
                act.wait_ge(s_o, f * NC + NC)
                if after_first(f):
                    act.wait_ge(f_x, f * 2)
                for half in range(2):
                    act.activation(osq[:, bass.ts(half, HALF)], po[:, half], ACT.Square).then_inc(f_sq, 1)

            def end_roots(f):
                for half in range(2):
                    act.wait_ge(f_nm, f * 2 + (half + 1))
                    act.activation(osq[:, bass.ts(half, HALF)], pp[:, half], ACT.Sqrt, scale=1.0 / P,
                                   bias=c["eps"][:, 0:1]).then_inc(f_rt, 1)

            def take_t(h, level):
                for b in range(4):
                    act.wait_ge(s_t, h * LT + (4 * level + b + 1))
                    act.activation(as_blocks(d[:, 2 * b:2 * b + 2].rearrange("p a n -> p (a n)"), LEVELS[level]),
                                   alternating(ring[:, b], 2 * P, 2 * P, LEVELS[level]), ACT.Copy).then_inc(s_td, 1)

            def take_w(h):
                for b in range(4):
                    act.wait_ge(s_w, h * 4 + (b + 1))
                    act.activation(wt[:, 4 * b:4 * b + 4], ring[:, b].rearrange("p (a n) -> p a n", n=P),
                                   ACT.Copy, scale=-1.0).then_inc(s_wd, 1)

            def slot(h, parity, more, before):
                g, q = h + 1, 1 - parity
                if more:
                    squares(g)
                if before:
                    end_squares(h - 1)
                take_t(h, 0)
                if more:
                    roots(g, 1)
                take_t(h, 1)
                if more:
                    roots(g, 0)
                if before:
                    end_roots(h - 1)
                take_t(h, 2)
                if more:
                    row_copies(g, 0)
                    column_exps(g, q)
                    row_exps(g)
                take_t(h, 3)
                if more:
                    row_copies(g, 1)
                    decays(g, 0, 5)
                take_t(h, 4)
                if more:
                    decays(g, 5, 5)
                take_t(h, 5)
                if more:
                    decays(g, 10, 6)
                take_w(h)

            squares(0)
            roots(0, 1)
            roots(0, 0)
            column_exps(0, 0)
            row_copies(0, 0)
            row_copies(0, 1)
            row_exps(0)
            decays(0, 0, NT)
            heads(act, slot)
            end_squares(A_HEADS - 1)
            end_roots(A_HEADS - 1)

        @block.gpsimd
        def _(pool):
            def neg_rows(g):
                pool.wait_ge(l_g, g * 16 + 16)
                if after_first(g):
                    pool.wait_ge(e_mt, g * 4 + M0)
                for direction in range(2):
                    pool.tensor_tensor(dec[:, direction * NC:(direction + 1) * NC],
                                       grow[:, direction].rearrange("p (a n) -> p a n", n=P),
                                       neg[:, direction, None, :].to_broadcast([P, NC, P]), ALU.add).then_inc(e_neg, 1)

            def beta_keys(g):
                pool.wait_ge(l_b, g * 16 + 16)
                pool.wait_ge(e_hat, g * 2 + (E0 + 1))
                for direction in range(2):
                    pool.tensor_tensor(brow[:, direction], qk[:, 1], brow[:, direction], ALU.mult).then_inc(e_kb, 1)

            def decayed_queries(g, parity):
                pool.wait_ge(e_eg, g * 2 + 2)
                pool.wait_ge(e_hat, g * 2 + (E0 + 2))
                if after_first(g - 1):
                    pool.wait_ge(s_o, g * NC - NC)
                for direction in range(2):
                    pool.tensor_tensor(qd[:, parity, direction * NC:(direction + 1) * NC],
                                       qk[:, 0].rearrange("p (a n) -> p a n", n=P),
                                       grow[:, direction].rearrange("p (a n) -> p a n", n=P), ALU.mult).then_inc(e_qd, 2)

            def scaled_rows(g, parity):
                pool.wait_ge(e_rows, g * 4 + 4)
                pool.wait_ge(e_ec, g * 3 + 3)
                pool.wait_ge(e_col, g * 3 + 3)
                for dst, src, scale in ((kbe, k_rows, beg), (kd, k_rows, kdc), (vb, v_rows, hb)):
                    for direction in range(2):
                        pool.tensor_tensor(dst[:, parity, direction * NC:(direction + 1) * NC], src[:],
                                           scale[:, direction, :, None].to_broadcast([P, NC, P]),
                                           ALU.mult).then_inc(e_scaled, 1)

            def first_inverse(g, parity):
                halves = [slice(direction * NC, (direction + 1) * NC) for direction in range(2)]
                for direction, half in enumerate(halves):
                    pool.wait_ge(e_mt, g * 4 + (M0 + 2 * direction + 2))
                    pool.tensor_tensor(dt[:, parity, half], mt[:, half],
                                       one_level[:, direction, None, :].to_broadcast([P, NC, P]), ALU.mult).then_inc(e_d1, 1)
                pool.wait_ge(e_d1, g * 4 + 2)
                for half in halves:
                    pool.tensor_tensor(dt[:, parity, half], dt[:, parity, half],
                                       ident[:, None, :].to_broadcast([P, NC, P]), ALU.add).then_inc(e_d1, 1)
                pool.tensor_tensor(mt[:, 0:NC], mt[:, 0:NC], mt[:, NC:NT], ALU.add).then_inc(e_both, 1)

            def prepare(g, parity):
                neg_rows(g)
                beta_keys(g)
                decayed_queries(g, parity)
                scaled_rows(g, parity)
                first_inverse(g, parity)

            prepare(0, 0)
            heads(pool, lambda h, parity, more, before: prepare(h + 1, 1 - parity) if more else None)

        @block.vector
        def _(dve):
            dve.sem_inc(e_hat, E0)
            dve.sem_inc(e_mt, M0)

            def columns(g):
                dve.wait_ge(l_g, g * 16 + 16)
                if after_first(g):
                    dve.wait_ge(e_scaled, g * 6)
                    dve.wait_ge(e_dec, g * NT)
                dve.tensor_copy(hc[:], cols[:, :, bass.ds(g, 1)].rearrange("p g a n -> p g (a n)")).then_inc(e_hc, 1)
                rows = grow[:].rearrange("p g (n i) -> p g n i", i=P)
                dve.tensor_copy(glast[:, 0], rows[:, 0, :, P - 1]).then_inc(e_gl, 1)
                dve.tensor_copy(glast[:, 1], rows[:, 1, :, 0]).then_inc(e_gl, 1)
                dve.wait_ge(e_gl, g * 2 + 2)
                dve.wait_ge(e_hc, g + 1)
                dve.tensor_tensor(kdc[:], glast[:], hc[:, 0:2], ALU.subtract).then_inc(e_dif, 1)
                dve.tensor_scalar(negc[:], hc[:, 0:2], -1.0, None, ALU.mult).then_inc(e_col, 1)
                dve.tensor_scalar(hb[:], hc[:, 2:4], 0.5, None, ALU.mult).then_inc(e_col, 1)

            def beta_column(g):
                dve.wait_ge(e_ec, g * 3 + 3)
                dve.tensor_tensor(beg[:], hc[:, 2:4], egc[:], ALU.mult).then_inc(e_col, 1)

            def unit(g, j):
                dve.wait_ge(e_rt, g * 4 + (2 * (1 - j) + 2))
                dve.reciprocal(root[:, j], root[:, j]).then_inc(e_rc, 1)
                dve.wait_ge(e_rc, g * 2 + (1 - j + 1))
                dve.scalar_tensor_tensor(qk[:, j], qk[:, j], 1.0 if j else float(P) ** -0.5, root[:, j],
                                         ALU.mult, ALU.mult).then_inc(e_hat, 1)

            def attention(g, parity):
                dve.wait_ge(e_dec, g * NT + NT)
                for half in range(2):
                    dve.wait_ge(e_qk, g * 2 + (half + 1))
                    for direction in range(2):
                        tiles = slice(direction * NC + 4 * half, direction * NC + 4 * half + 4)
                        dve.tensor_tensor(pt[:, parity, tiles], pp[:, half].rearrange("p (a n) -> p a n", n=P),
                                          dec[:, tiles], ALU.mult).then_inc(e_pt, 1)

            def matrix(g, b):
                tiles = slice(4 * b, 4 * b + 4)
                dve.wait_ge(e_g, g * 4 + (b + 1))
                dve.wait_ge(e_dec, g * NT + NT)
                dve.scalar_tensor_tensor(mt[:, tiles], pp[:, b % 2].rearrange("p (a n) -> p a n", n=P), -1.0,
                                         dec[:, tiles], ALU.mult, ALU.mult).then_inc(e_mt, 1)

            def take_z(h, level, b):
                dve.wait_ge(s_z, h * LZ + (4 * level + b + 1))
                dve.tensor_tensor(zz[:, 2 * b:2 * b + 2], ring[:, b, 0:2 * P].rearrange("p (a n) -> p a n", n=P),
                                  masks[:, level, None, :].to_broadcast([P, 2, P]), ALU.mult).then_inc(s_zd, 1)

            def take_i(h, parity, level, b):
                dve.wait_ge(s_i, h * LZ + (4 * level + b + 1))
                left = left_d(parity, 2 * b, 2, level)
                dve.tensor_tensor(left, as_blocks(ring[:, b, 0:2 * P], LEVELS[level]), left, ALU.add).then_inc(s_id, 1)

            def end_reciprocal(f):
                dve.wait_ge(f_rt, f * 2 + 2)
                dve.reciprocal(osq[:], osq[:]).then_inc(f_rc, 1)

            def end(f, parity):
                dve.wait_ge(l_on, 16)
                if after_first(f):
                    dve.wait_ge(f_st, f * 16)
                dve.wait_ge(f_rc, f + 1)
                for half in range(2):
                    dve.scalar_tensor_tensor(fin[:, bass.ts(half, HALF)], po[:, half], onorm[:, 0:1],
                                             osq[:, bass.ts(half, HALF)], ALU.mult, ALU.mult).then_inc(f_x, 1)
                dve.wait_ge(f_x, f * 2 + 2)
                dve.wait_ge(l_z, f * 16 + 16)
                dve.scalar_tensor_tensor(fin[:], fin[:], 0.5, z[:, parity], ALU.mult, ALU.mult).then_inc(f_res, 1)

            def scan_step(h, parity, t):
                dve.wait_ge(s_vn, h * NC + (t + 1))
                dve.tensor_copy(vnew[:, t % 2],
                                ring[:, t % 2, 0:2 * P].rearrange("p (a n) -> p a n", n=P)).then_inc(s_vd, 1)
                if t == NC - 1:
                    return
                dve.wait_ge(s_s, h * (NC - 1) + (t + 1))
                if t > 0:
                    dve.wait_ge(s_sd, h * KS + (2 * t))
                for direction in range(2):
                    inc = ring[:, 2 + t % 2, bass.ts(direction, P)]
                    chunk = chunk_of(direction, t)
                    new = state[:, (t + 1) % 2, direction]
                    if t == 0:
                        dve.tensor_copy(new, inc).then_inc(s_sd, 1)
                    else:
                        dve.scalar_tensor_tensor(new, state[:, t % 2, direction],
                                                 cdec[:, parity, direction, chunk:chunk + 1], inc,
                                                 ALU.mult, ALU.add).then_inc(s_sd, 1)

            def slot(h, parity, more, before):
                g, q = h + 1, 1 - parity
                for level in range(L):
                    for b in range(4):
                        take_z(h, level, b)
                    if more and level == 0:
                        columns(g)
                    if more and level == 1:
                        unit(g, 1)
                    if more and level == 3:
                        beta_column(g)
                    for b in range(4):
                        take_i(h, parity, level, b)
                    if more and level == 1:
                        unit(g, 0)
                    if before and level == 2:
                        end_reciprocal(h - 1)
                        end(h - 1, q)
                if more:
                    attention(g, q)
                    matrix(g, 0)
                    matrix(g, 1)
                for t in range(NC):
                    scan_step(h, parity, t)
                    if more and t == 3:
                        matrix(g, 2)
                        matrix(g, 3)

            columns(0)
            unit(0, 1)
            unit(0, 0)
            beta_column(0)
            attention(0, 0)
            for b in range(4):
                matrix(0, b)
            heads(dve, slot)
            end_reciprocal(A_HEADS - 1)
            end(A_HEADS - 1, 1)

        @block.tensor
        def _(pe):
            def norm_sums(g, j):
                for half in range(2):
                    pe.wait_ge(e_sq, g * 2 + (1 - j + 1))
                    if j == 1:
                        pe.wait_ge(e_mt, g * 4 + M0)
                    else:
                        pe.wait_ge(e_rt, g * 4 + (half + 1))
                    pe.matmul(pp[:, half], c["ones"][:], root[:, j, bass.ts(half, HALF)],
                              start=True, stop=True).then_inc(e_nm, 1)

            def to_rows(g, which, before):
                if which == 0:
                    pe.wait_ge(e_hat, g * 2 + (E0 + 2))
                    if before is not None:
                        pe.wait_ge(f_rt, before * 2 + 2)
                else:
                    pe.wait_ge(l_v, g * 16 + 16)
                src = v[:] if which else qk[:, 1]
                for half in range(2):
                    if which:
                        pe.wait_ge(e_rows, g * 4 + (half + 1))
                    for i in range(4):
                        last = pe.transpose(pp[:, half, bass.ts(i, P)], src[:, bass.ts(4 * half + i, P)], ident[:])
                    last.then_inc(e_tr, 1)

            def queries_keys(g):
                for half in range(2):
                    pe.wait_ge(e_rows, g * 4 + (half + 3))
                    for i in range(4):
                        cols_ = bass.ts(4 * half + i, P)
                        last = pe.matmul(pp[:, half, bass.ts(i, P)], qk[:, 1, cols_], qk[:, 0, cols_],
                                         start=True, stop=True)
                    last.then_inc(e_qk, 1)

            def keys_keys(g, b):
                direction, half = divmod(b, 2)
                pe.wait_ge(e_kb, g * 2 + (direction + 1))
                if b < 2:
                    pe.wait_ge(e_pt, g * 4 + (2 * half + 2))
                else:
                    pe.wait_ge(e_mt, g * 4 + (M0 + b - 1))
                for i in range(4):
                    cols_ = bass.ts(4 * half + i, P)
                    last = pe.matmul(pp[:, half, bass.ts(i, P)], qk[:, 1, cols_], brow[:, direction, cols_],
                                     start=True, stop=True)
                last.then_inc(e_g, 1)

            def end_sums(f, bank_free, count):
                pe.wait_ge(bank_free, count)
                for half in range(2):
                    pe.wait_ge(f_sq, f * 2 + (half + 1))
                    pe.matmul(pp[:, half], c["ones"][:], osq[:, bass.ts(half, HALF)],
                              start=True, stop=True).then_inc(f_nm, 1)

            def transposes(h, parity, level, b):
                if level == 0:
                    pe.wait_ge(e_d1, h * 4 + 4)
                    if after_first(h):
                        pe.wait_ge(s_vd, h * NC)
                        pe.wait_ge(s_sd, h * KS)
                else:
                    pe.wait_ge(s_id, h * LZ + (4 * (level - 1) + b + 1))
                for i in range(4):
                    last = pe.transpose(ring[:, b, bass.ts(i, P)], dt[:, parity, i // 2 * NC + 2 * b + i % 2], ident[:])
                last.then_inc(s_t, 1)

            def products_z(h, level, b):
                pe.wait_ge(s_td, h * LT + (4 * level + b + 1))
                if level == 0 and b == 0:
                    pe.wait_ge(e_both, h + 1)
                for i in range(2):
                    last = pe.matmul(ring[:, b, bass.ts(i, P)], mt[:, 2 * b + i], d[:, 2 * b + i], start=True, stop=True)
                last.then_inc(s_z, 1)

            def products_i(h, parity, level, b):
                pe.wait_ge(s_zd, h * LZ + (4 * level + b + 1))
                for i in range(2):
                    last = pe.matmul(as_blocks(ring[:, b, bass.ts(i, P)], LEVELS[level]), zz[:, 2 * b + i],
                                     left_d(parity, 2 * b + i, 1, level), start=True, stop=True)
                last.then_inc(s_i, 1)

            def products_w(h, parity, b):
                pe.wait_ge(s_id, h * LZ + (4 * (L - 1) + 2 * (b % 2) + 2))
                if b == 0:
                    pe.wait_ge(e_scaled, h * 6 + 6)
                for i in range(4):
                    last = pe.matmul(ring[:, b, bass.ts(i, P)], kbe[:, parity, 4 * b + i], dt[:, parity, 4 * b + i],
                                     start=True, stop=True)
                last.then_inc(s_w, 1)

            def scan_step(h, parity, t):
                if t == 0:
                    pe.wait_ge(s_wd, h * 4 + 4)
                    pe.wait_ge(e_qd, h * 4 + 4)
                    pe.wait_ge(e_pt, h * 4 + 4)
                    if after_first(h):
                        pe.wait_ge(f_x, h * 2)
                if t >= 2:
                    pe.wait_ge(s_vd, h * NC + (t - 1))
                for direction in range(2):
                    tile = direction * NC + chunk_of(direction, t)
                    out = ring[:, t % 2, bass.ts(direction, P)]
                    last = pe.matmul(out, dt[:, parity, tile], vb[:, parity, tile], start=direction == 0, stop=False,
                                     skip_group_check=True)
                if t > 0:
                    pe.wait_ge(s_sd, h * KS + 2 * t)
                    for direction in range(2):
                        tile = direction * NC + chunk_of(direction, t)
                        last = pe.matmul(ring[:, t % 2, bass.ts(direction, P)], wt[:, tile], state[:, t % 2, direction],
                                         start=False, stop=direction == 1, skip_group_check=True)
                last.then_inc(s_vn, 1)
                if t > 0:
                    for direction in range(2):
                        chunk = chunk_of(direction, t)
                        pe.matmul(po[:, chunk // 4, bass.ts(chunk % 4, P)], state[:, t % 2, direction],
                                  qd[:, parity, direction * NC + chunk], start=False, stop=False, skip_group_check=True)
                pe.wait_ge(s_vd, h * NC + (t + 1))
                if t < NC - 1:
                    for direction in range(2):
                        tile = direction * NC + chunk_of(direction, t)
                        last = pe.matmul(ring[:, 2 + t % 2, bass.ts(direction, P)], kd[:, parity, tile],
                                         vnew[:, t % 2, direction], start=True, stop=True)
                    last.then_inc(s_s, 1)
                for direction in range(2):
                    chunk = chunk_of(direction, t)
                    last = pe.matmul(po[:, chunk // 4, bass.ts(chunk % 4, P)], vnew[:, t % 2, direction],
                                     pt[:, parity, direction * NC + chunk], start=t == 0, stop=t == NC - 1,
                                     skip_group_check=True)
                last.then_inc(s_o, 1)

            def slot(h, parity, more, before):
                g, q = h + 1, 1 - parity
                for b in range(4):
                    transposes(h, parity, 0, b)
                for level in range(L):
                    for b in range(4):
                        products_z(h, level, b)
                    if more and level == 0:
                        norm_sums(g, 1)
                    if more and level == 2:
                        to_rows(g, 0, h - 1 if before else None)
                    if more and level == 4:
                        queries_keys(g)
                    if before and level == 1:
                        if more:
                            end_sums(h - 1, e_rt, g * 4 + 4)
                        else:
                            end_sums(h - 1, e_mt, A_HEADS * 4 + M0)
                    for b in range(4):
                        products_i(h, parity, level, b)
                    if more and level == 0:
                        norm_sums(g, 0)
                    if more and level == 2:
                        to_rows(g, 1, None)
                    if level < L - 1:
                        for b in range(4):
                            transposes(h, parity, level + 1, b)
                for b in range(4):
                    products_w(h, parity, b)
                if more:
                    keys_keys(g, 0)
                    keys_keys(g, 1)
                for t in range(NC):
                    scan_step(h, parity, t)
                    if more and t in (2, 3):
                        keys_keys(g, t)

            norm_sums(0, 1)
            norm_sums(0, 0)
            to_rows(0, 0, None)
            to_rows(0, 1, None)
            queries_keys(0)
            for b in range(4):
                keys_keys(0, b)
            heads(pe, slot)
            end_sums(A_HEADS - 1, f_rt, 2 * (A_HEADS - 1))

def attention_stage(nc, c, proj, kv_scratch, consts, mixed):
    BLK, W = SEQ // P, 3 * P
    U = 5
    LAST = U - 1
    with ExitStack() as stack:
        n = Names(nc, stack, "at_")
        cos, sin = n.sb("cos", [P, SEQ]), n.sb("sin", [P, SEQ])
        qw, kw, cw_, nsink = n.sb("qw", [P, 1]), n.sb("kw", [P, 1]), n.sb("cw", [P, 1]), n.sb("nsink", [P, 2, 4])
        rot, rot_q, half_ones, pair_ones = (n.sb("rot", [P, P]), n.sb("rot_q", [P, P]), n.sb("half_ones", [P, 2]),
                                            n.sb("pair_ones", [P, P]))
        qcos, window = n.sb("qcos", [P, SEQ]), n.sb("window", [P, 3, W])
        tile_in, squares = n.sb("tile_in", [P, 2, SEQ]), n.sb("squares", [P, 2, SEQ])
        k_in, v_in, k_tmp = n.sb("k_in", [P, SEQ]), n.sb("v_in", [P, SEQ]), n.sb("k_tmp", [P, SEQ])
        k_pad = n.sb("k_pad", [P, 2, SEQ + 2 * P])
        v_rows = n.sb("v_rows", [P, BLK + 2, P])
        v_win = n.sb("v_win", [P, 2, 3, P])
        kv, mem_k = n.sb("kv", [P, 2, 2, HALF]), n.sb("mem_k", [P, C_HEADS, MEM_LEN])
        rq = n.sb("rq", [P, BLK, 12])
        q_in, z_in = n.sb("q_in", [P, 2, 8, P]), n.sb("z_in", [P, 2, 8, P])
        q_rope, q_tmp, q_mem = n.sb("q_rope", [P, 2, 4, P]), n.sb("q_tmp", [P, 4, P]), n.sb("q_mem", [P, 2, 4, P])
        sm = n.sb("sm", [P, 2, 2, W])
        prob = n.sb("prob", [P, 2, SEQ])
        mx, negm, rsum, diff, sinks = (n.sb(x, [P, 2, 4]) for x in ("mx", "negm", "rsum", "diff", "sinks"))
        pt_b, pt_c = n.sb("pt_b", [P, 3, 2, 4, P]), n.sb("pt_c", [P, 2, C_HEADS, P])
        out_b, out_c = n.sb("out_b", [P, 4, P]), n.sb("out_c", [P, 4, P])
        ps = n.ps("ps", [P, 2, 2, HALF])
        tp, po, px = n.ps("tp", [P, 2, HALF]), n.ps("po", [P, HALF]), n.ps("px", [P, HALF])

        l_c, l_k, l_v, l_kv, l_q, l_z = (n.sem(x) for x in ("l_c", "l_k", "l_v", "l_kv", "l_q", "l_z"))
        l_t = [n.sem(f"l_t{i}") for i in range(2)]
        p_zero, p_w, p_sq, p_sum, p_root, p_rq = (n.sem(x) for x in ("p_zero", "p_w", "p_sq", "p_sum", "p_root", "p_rq"))
        k_sq, k_sum, k_root, k_rc, k_n, k_rot, k_out, k_v, k_vd, k_mt, k_mk = (
            n.sem(x) for x in ("k_sq", "k_sum", "k_root", "k_rc", "k_n", "k_rot", "k_out", "k_v", "k_vd", "k_mt", "k_mk"))
        b_win, b_rot, b_q, b_mem = (n.sem(x) for x in ("b_win", "b_rot", "b_q", "b_mem"))
        b_s, b_a, b_m, b_n, b_e, b_es, b_d, b_p = (
            n.sem(x) for x in ("b_s", "b_a", "b_m", "b_n", "b_e", "b_es", "b_d", "b_p"))
        b_t, b_td, b_o, b_res = (n.sem(x) for x in ("b_t", "b_td", "b_o", "b_res"))
        st_b, st_c = n.sem("st_b"), n.sem("st_c")
        block = stack.enter_context(nc.Block())
        AHEAD = 2

        def blocks(eng, slot):
            slot(0, 0, True, 0)
            slot(1, 1, True, 1)
            with eng.Fori(1, BLK // 2 - 1) as i:
                slot(i * 2, 0, True, 1)
                slot(i * 2 + 1, 1, True, 1)
            slot(BLK - 2, 0, True, 1)
            slot(BLK - 1, 1, False, 2)

        def after(h, k):
            return not isinstance(h, int) or h >= k

        def proj_block(first, h):
            return proj[first:first + 4, :, bass.ds(h * P, P)].rearrange("a p n -> p a n")

        @block.sync
        def _(sp):
            loads = [(cos, consts["cos"]), (sin, consts["sin"]), (qw, consts["qw"]), (kw, consts["kw"]),
                     (cw_, consts["cw"]), (nsink, consts["sink"]), (rot, consts["rot"]),
                     (half_ones, consts["half_ones"]), (pair_ones, consts["pair_ones"]), (window, consts["window"])]
            for dst, src in loads:
                sp.dma_start(dst[:], src).then_inc(l_c, 16)
            sp.dma_start(k_in[:], proj[T_BK]).then_inc(l_k, 16)
            sp.dma_start(v_in[:], proj[T_BV]).then_inc(l_v, 16)
            sp.dma_start(kv[:], kv_scratch).then_inc(l_kv, 16)
            for i in range(8):
                if i >= 2:
                    sp.wait_ge(p_sq, i - 1)
                sp.dma_start(tile_in[:, i % 2], proj[T_BQ + i if i < 4 else T_CQ + i - 4]).then_inc(l_t[i % 2], 16)

            def load(h, parity):
                if after(h, 1):
                    sp.wait_ge(l_q, h * 32)
                    sp.wait_ge(l_z, h * 32)
                if after(h, 2):
                    sp.wait_ge(b_q, h * 3 - 3)
                    sp.wait_ge(b_mem, h - 1)
                    sp.wait_ge(b_res, h * 2 - 2)
                sp.dma_start(q_in[:, parity, 0:4], proj_block(T_BQ, h)).then_inc(l_q, 16)
                sp.dma_start(q_in[:, parity, 4:8], proj_block(T_CQ, h)).then_inc(l_q, 16)
                sp.dma_start(z_in[:, parity, 0:4], proj_block(T_BZ, h)).then_inc(l_z, 16)
                sp.dma_start(z_in[:, parity, 4:8], proj_block(T_CZ, h)).then_inc(l_z, 16)

            load(0, 0)
            blocks(sp, lambda h, parity, more, w: load(h + 1, 1 - parity) if more else None)

        @block.gpsimd
        def _(pool):
            pool.memset(k_pad[:], 0.0).then_inc(p_zero, 1)
            pool.memset(v_rows[:, 0], 0.0).then_inc(p_zero, 1)
            pool.memset(v_rows[:, BLK + 1], 0.0).then_inc(p_zero, 1)
            pool.wait_ge(k_vd, 2)
            pool.wait_ge(p_zero, 3)

            def slot(h, parity, more, w):
                if after(h, 2):
                    pool.wait_ge(b_o, h * 2 - 2)
                pool.tensor_copy(v_win[:, parity], v_rows[:, bass.ds(h, 3)]).then_inc(b_win, 1)
                pool.wait_ge(b_res, h * 2 + 1)
                pool.dma_start(mixed[A_HEADS:A_HEADS + 4, :, bass.ds(h * P, P)].rearrange("a p n -> p a n"),
                               out_b[:]).then_inc(st_b, 16)
                pool.wait_ge(b_res, h * 2 + 2)
                pool.dma_start(mixed[A_HEADS + 4:A_HEADS + 8, :, bass.ds(h * P, P)].rearrange("a p n -> p a n"),
                               out_c[:]).then_inc(st_c, 16)

            blocks(pool, slot)
            pool.wait_ge(st_b, 16 * BLK)
            pool.wait_ge(st_c, 16 * BLK)

        @block.scalar
        def _(act):
            act.wait_ge(l_k, 16)
            act.activation(k_tmp[:], k_in[:], ACT.Square).then_inc(k_sq, 1)
            for i in range(8):
                act.wait_ge(l_t[i % 2], 16 * (i // 2 + 1))
                if i >= 2:
                    act.wait_ge(p_sum, i - 1)
                act.activation(squares[:, i % 2], tile_in[:, i % 2], ACT.Square).then_inc(p_sq, 1)
            for half in range(2):
                act.wait_ge(k_sum, half + 1)
                act.activation(k_tmp[:, bass.ts(half, HALF)], ps[:, 0, half], ACT.Sqrt, scale=1.0 / B_DIM,
                               bias=c["eps"][:, 0:1]).then_inc(k_root, 1)
            act.wait_ge(p_sum, 8)
            sums = px[:, 0:BLK * 12].rearrange("p (b t) -> p b t", t=12)
            act.activation(rq[:, :, 0:8], sums[:, :, 0:8], ACT.Sqrt, bias=c["eps64"][:, 0:1]).then_inc(p_root, 1)
            act.activation(rq[:, :, 8:12], sums[:, :, 8:12], ACT.Sqrt, bias=c["eps128"][:, 0:1]).then_inc(p_root, 1)
            for half in range(2):
                act.wait_ge(k_v, half + 1)
                act.activation(v_rows[:, 1 + 4 * half:5 + 4 * half], tp[:, half].rearrange("p (a n) -> p a n", n=P),
                               ACT.Copy).then_inc(k_vd, 1)
            for m in range(2):
                act.wait_ge(k_mt, m + 1)
                act.activation(mem_k[:, :, bass.ts(m, P)], ps[:, 1, m].rearrange("p (a n) -> p a n", n=P),
                               ACT.Copy).then_inc(k_mk, 1)

            def exps(h, u, odd, parity):
                if u < LAST:
                    act.wait_ge(b_n, h * 9 + (2 * u + 2))
                    if not (isinstance(h, int) and h == 0 and u < 2):
                        act.wait_ge(b_t, h * 10 + (2 * u - 2))
                    for i in range(2):
                        act.activation(prob[:, odd, i * W:i * W + W], sm[:, odd, i], ACT.Exp,
                                       bias=negm[:, odd, i:i + 1], accum_out=rsum[:, odd, i:i + 1]).then_inc(b_e, 1)
                    act.activation(sinks[:, odd, 0:2], diff[:, odd, 0:2], ACT.Exp).then_inc(b_es, 1)
                else:
                    act.wait_ge(b_n, h * 9 + 9)
                    act.wait_ge(b_t, h * 10 + 6)
                    for i in range(4):
                        act.activation(prob[:, odd, i * MEM_LEN:(i + 1) * MEM_LEN],
                                       ps[:, odd, i // 2, bass.ts(i % 2, MEM_LEN)], ACT.Exp,
                                       bias=negm[:, odd, i:i + 1], scale=rq[:, bass.ds(h, 1), 8 + i],
                                       accum_out=rsum[:, odd, i:i + 1]).then_inc(b_e, 1)

            def take_t(h, u):
                if u == 0 and after(h, 1):
                    act.wait_ge(b_o, h * 2 - 1)
                if u == LAST and after(h, 1):
                    act.wait_ge(b_o, h * 2)
                for i in range(2):
                    act.wait_ge(b_t, h * 10 + (2 * u + i + 1))
                    if u < LAST:
                        act.activation(pt_b[:, :, i, u], tp[:, i, 0:W].rearrange("p (a n) -> p a n", n=P),
                                       ACT.Copy).then_inc(b_td, 1)
                    else:
                        act.activation(pt_c[:, i], tp[:, i].rearrange("p (a n) -> p a n", n=P),
                                       ACT.Copy).then_inc(b_td, 1)

            def slot(h, parity, more, w):
                for u in range(U):
                    if u < LAST:
                        exps(h, u + 1, (parity + u + 1) % 2, parity)
                    elif more:
                        exps(h + 1, 0, (parity + U) % 2, 1 - parity)
                    take_t(h, u)

            exps(0, 0, 0, 0)
            blocks(act, slot)

        @block.vector
        def _(dve):
            dve.wait_ge(l_c, 160)
            dve.tensor_scalar(nsink[:], nsink[:], -1.0, None, ALU.mult).then_inc(p_w, 1)
            dve.tensor_scalar(rot_q[:], rot[:], qw[:, 0:1], None, ALU.mult).then_inc(p_w, 1)
            dve.tensor_scalar(qcos[:], cos[:], qw[:, 0:1], None, ALU.mult).then_inc(p_w, 1)
            dve.wait_ge(k_root, 2)
            dve.reciprocal(k_tmp[:], k_tmp[:]).then_inc(k_rc, 1)
            dve.wait_ge(k_rc, 1)
            dve.scalar_tensor_tensor(k_in[:], k_in[:], kw[:, 0:1], k_tmp[:], ALU.mult, ALU.mult).then_inc(k_n, 1)
            dve.wait_ge(k_n, 1)
            for half in range(2):
                cols_ = bass.ts(half, HALF)
                dve.wait_ge(k_rot, half + 1)
                dve.tensor_tensor(k_tmp[:, cols_], ps[:, 0, half], sin[:, cols_], ALU.mult).then_inc(k_n, 1)
            dve.tensor_tensor(k_in[:], k_in[:], cos[:], ALU.mult).then_inc(k_n, 1)
            dve.wait_ge(k_n, 4)
            dve.wait_ge(p_zero, 1)
            for g in range(2):
                rows = slice(64 * g, 64 * g + 64)
                dve.tensor_tensor(k_pad[rows, g, P:P + SEQ], k_in[rows, :], k_tmp[rows, :], ALU.add).then_inc(k_out, 1)
            dve.wait_ge(p_root, 2)
            dve.reciprocal(rq[:], rq[:]).then_inc(p_rq, 1)
            dve.wait_ge(p_rq, 1)
            dve.wait_ge(p_w, 3)

            def queries(h, parity):
                dve.wait_ge(l_q, h * 32 + 32)
                if after(h, 1):
                    dve.wait_ge(b_q, h * 3)
                if after(h, 2):
                    dve.wait_ge(b_s, h * U - U)
                at = bass.ds(h * P, P)
                dve.tensor_tensor(q_rope[:, parity], q_in[:, parity, 0:4],
                                  qcos[:, None, at].to_broadcast([P, 4, P]), ALU.mult).then_inc(b_q, 1)
                dve.tensor_scalar(q_mem[:, parity], q_in[:, parity, 4:8], cw_[:, 0:1], None, ALU.mult).then_inc(b_mem, 1)
                dve.wait_ge(b_rot, h + 1)
                dve.tensor_tensor(q_tmp[:], px[:].rearrange("p (a n) -> p a n", n=P),
                                  sin[:, None, at].to_broadcast([P, 4, P]), ALU.mult).then_inc(b_q, 1)
                dve.wait_ge(b_q, h * 3 + 2)
                dve.tensor_tensor(q_rope[:, parity], q_rope[:, parity], q_tmp[:], ALU.add).then_inc(b_q, 1)

            def maxima(h, u, odd, which):
                dve.wait_ge(b_s, h * U + (u + 1))
                if not (isinstance(h, int) and h == 0 and u < 2):
                    dve.wait_ge(b_e, h * 12 + (-4, 0, 2, 4, 6)[u])
                    dve.wait_ge(b_es, h * 4 + (0, 0, 1, 2, 3)[u])
                if u < LAST:
                    for i in range(2):
                        dve.scalar_tensor_tensor(sm[:, odd, i], ps[:, odd, i, 0:W], rq[:, bass.ds(h, 1), 2 * u + i],
                                                 window[:, which], ALU.mult, ALU.add).then_inc(b_a, 1)
                    dve.wait_ge(b_a, h * 8 + (2 * u + 2))
                    dve.tensor_reduce(mx[:, odd, 0:2], sm[:, odd], AX_X, ALU.max).then_inc(b_m, 1)
                    dve.wait_ge(b_m, h * 6 + (u + 1))
                    dve.scalar_tensor_tensor(negm[:, odd, 0:2], mx[:, odd, 0:2], -1.0, nsink[:, :, u],
                                             ALU.mult, ALU.min).then_inc(b_n, 1)
                    dve.wait_ge(b_n, h * 9 + (2 * u + 1))
                    dve.tensor_tensor(diff[:, odd, 0:2], negm[:, odd, 0:2], nsink[:, :, u], ALU.subtract).then_inc(b_n, 1)
                else:
                    dve.tensor_reduce(mx[:, odd].rearrange("p (b a) -> p b a", b=2), ps[:, odd].rearrange("p b (a n) -> p b a n", n=MEM_LEN),
                                      AX_X, ALU.max).then_inc(b_m, 1)
                    dve.wait_ge(b_m, h * 6 + 5)
                    dve.tensor_scalar(mx[:, odd], mx[:, odd], -1.0, None, ALU.mult).then_inc(b_m, 1)
                    dve.wait_ge(b_m, h * 6 + 6)
                    dve.tensor_tensor(negm[:, odd], mx[:, odd], rq[:, bass.ds(h, 1), 8:12].rearrange("p a t -> p (a t)"),
                                      ALU.mult).then_inc(b_n, 1)

            def probabilities(h, u, odd):
                if u < LAST:
                    dve.wait_ge(b_e, h * 12 + (2 * u + 2))
                    dve.wait_ge(b_es, h * 4 + (u + 1))
                    dve.tensor_tensor(rsum[:, odd, 0:2], rsum[:, odd, 0:2], sinks[:, odd, 0:2], ALU.add).then_inc(b_d, 1)
                    dve.wait_ge(b_d, h * 9 + (2 * u + 1))
                    dve.reciprocal(rsum[:, odd, 0:2], rsum[:, odd, 0:2]).then_inc(b_d, 1)
                    dve.wait_ge(b_d, h * 9 + (2 * u + 2))
                    for i in range(2):
                        part = prob[:, odd, i * W:i * W + W]
                        dve.tensor_scalar(part, part, rsum[:, odd, i:i + 1], None, ALU.mult).then_inc(b_p, 1)
                else:
                    dve.wait_ge(b_e, h * 12 + 12)
                    dve.reciprocal(rsum[:, odd], rsum[:, odd]).then_inc(b_d, 1)
                    dve.wait_ge(b_d, h * 9 + 9)
                    for i in range(4):
                        part = prob[:, odd, i * MEM_LEN:(i + 1) * MEM_LEN]
                        dve.tensor_scalar(part, part, rsum[:, odd, i:i + 1], None, ALU.mult).then_inc(b_p, 1)

            def results(h, parity, which):
                out, st = ((out_b, st_b), (out_c, st_c))[which]
                dve.wait_ge(b_o, h * 2 + (which + 1))
                dve.wait_ge(l_z, h * 32 + 32)
                if after(h, 1):
                    dve.wait_ge(st, h * 16)
                dve.scalar_tensor_tensor(out[:], po[:].rearrange("p (a n) -> p a n", n=P), 0.5,
                                         z_in[:, parity, 4 * which:4 * which + 4], ALU.mult, ALU.mult).then_inc(b_res, 1)

            def slot(h, parity, more, w):
                for u in range(U):
                    if u < LAST:
                        maxima(h, u + 1, (parity + u + 1) % 2, w)
                    elif more:
                        maxima(h + 1, 0, (parity + U) % 2, NEXT_WINDOW(h))
                    probabilities(h, u, (parity + u) % 2)
                    if more and u == 0:
                        queries(h + 1, 1 - parity)
                results(h, parity, 0)
                results(h, parity, 1)

            def NEXT_WINDOW(h):
                return 2 if isinstance(h, int) and h == BLK - 2 else 1

            queries(0, 0)
            maxima(0, 0, 0, 0)
            blocks(dve, slot)

        @block.tensor
        def _(pe):
            pe.wait_ge(l_c, 160)
            for half in range(2):
                pe.wait_ge(k_sq, 1)
                pe.matmul(ps[:, 0, half], pair_ones[:], k_tmp[:, bass.ts(half, HALF)], start=True, stop=True).then_inc(k_sum, 1)
            for half in range(2):
                pe.wait_ge(l_v, 16)
                for i in range(4):
                    last = pe.transpose(tp[:, half, bass.ts(i, P)], v_in[:, bass.ts(4 * half + i, P)], c["ident"][:])
                last.then_inc(k_v, 1)
            pe.wait_ge(l_kv, 16)
            for m in range(2):
                for i in range(C_HEADS):
                    last = pe.transpose(ps[:, 1, m, bass.ts(i, P)], kv[:, m, 0, bass.ts(i, P)], c["ident"][:])
                last.then_inc(k_mt, 1)
            for i in range(8):
                pe.wait_ge(p_sq, i + 1)
                for b in range(BLK):
                    cols_ = slice(12 * b + 2 * i, 12 * b + 2 * i + 2) if i < 4 else slice(12 * b + 4 + i, 12 * b + 5 + i)
                    last = pe.matmul(px[:, cols_], squares[:, i % 2, bass.ts(b, P)],
                                     half_ones[:] if i < 4 else c["ones"][:, 0:1], start=True, stop=True)
                last.then_inc(p_sum, 1)
            pe.wait_ge(k_n, 1)
            pe.wait_ge(k_root, 2)
            for half in range(2):
                pe.matmul(ps[:, 0, half], rot[:], k_in[:, bass.ts(half, HALF)], start=True, stop=True).then_inc(k_rot, 1)
            pe.wait_ge(k_out, 2)
            pe.wait_ge(k_mk, 2)
            pe.wait_ge(k_vd, 2)
            pe.wait_ge(p_w, 3)
            pe.wait_ge(p_rq, 1)

            def rotate(h, parity):
                pe.wait_ge(l_q, h * 32 + 32)
                if after(h, 1):
                    pe.wait_ge(b_q, h * 3)
                pe.matmul(px[:], rot_q[:], q_in[:, parity, 0:4].rearrange("p a n -> p (a n)"),
                          start=True, stop=True).then_inc(b_rot, 1)

            def scores(h, u, odd, parity):
                if not (isinstance(h, int) and h == 0 and u < 2):
                    if u in (1,):
                        pe.wait_ge(b_e, h * 12)
                    else:
                        pe.wait_ge(b_a, h * 8 + {0: 0, 2: 2, 3: 4, 4: 6}[u])
                if u < LAST:
                    if u == 0:
                        pe.wait_ge(b_q, h * 3 + 3)
                    for g in range(2):
                        last = pe.matmul(ps[:, odd, g, 0:W], q_rope[:, parity, u], k_pad[:, g, bass.ds(h * P, W)],
                                         start=True, stop=True)
                else:
                    pe.wait_ge(b_mem, h + 1)
                    for i in range(C_HEADS):
                        last = pe.matmul(ps[:, odd, i // 2, bass.ts(i % 2, MEM_LEN)], q_mem[:, parity, i], mem_k[:, i],
                                         start=True, stop=True)
                last.then_inc(b_s, 1)

            def transposes(h, u, odd):
                for i in range(2):
                    if u < LAST:
                        pe.wait_ge(b_p, h * 12 + (2 * u + i + 1))
                    else:
                        pe.wait_ge(b_p, h * 12 + 12)
                    if not (isinstance(h, int) and h == 0 and u == 0):
                        pe.wait_ge(b_td, h * 10 + (2 * u + i - 1))
                    if u < LAST:
                        for kc in range(3):
                            last = pe.transpose(tp[:, i, bass.ts(kc, P)], prob[:, odd, i * W + kc * P:i * W + (kc + 1) * P],
                                                c["ident"][:])
                    else:
                        for head in range(C_HEADS):
                            at = head * MEM_LEN + i * P
                            last = pe.transpose(tp[:, i, bass.ts(head, P)], prob[:, odd, at:at + P], c["ident"][:])
                    last.then_inc(b_t, 1)

            def values(h, parity):
                pe.wait_ge(b_td, h * 10 + 8)
                pe.wait_ge(b_win, h + 1)
                if after(h, 1):
                    pe.wait_ge(b_res, h * 2)
                for kc in range(3):
                    for g in range(2):
                        last = pe.matmul(po[64 * g:64 * g + 64, :], v_win[:, parity, kc, 64 * g:64 * g + 64],
                                         pt_b[:, kc, g].rearrange("p a n -> p (a n)"), start=kc == 0, stop=kc == 2)
                last.then_inc(b_o, 1)
                pe.wait_ge(b_td, h * 10 + 10)
                pe.wait_ge(b_res, h * 2 + 1)
                for head in range(C_HEADS):
                    for m in range(2):
                        last = pe.matmul(po[:, bass.ts(head, P)], kv[:, m, 1, bass.ts(head, P)], pt_c[:, m, head],
                                         start=m == 0, stop=m == 1)
                last.then_inc(b_o, 1)

            def slot(h, parity, more, w):
                for u in range(U):
                    if u + AHEAD < U:
                        scores(h, u + AHEAD, (parity + u) % 2, parity)
                    elif more:
                        scores(h + 1, u + AHEAD - U, (parity + u) % 2, 1 - parity)
                    transposes(h, u, (parity + u) % 2)
                    if more and u == 0:
                        rotate(h + 1, 1 - parity)
                values(h, parity)

            rotate(0, 0)
            scores(0, 0, 0, 0)
            scores(0, 1, 1, 0)
            blocks(pe, slot)


def output_stage(nc, c, mixed, w_out, x, out):
    FT, QUART = D_MODEL // P, 4
    NQ, NS, GROUP = FT // QUART, D_MODEL // HALF, 4
    with ExitStack() as stack:
        n = Names(nc, stack, "ou_")
        m_hi, m_lo = n.sb("m_hi", [P, FT, SEQ], F32R), n.sb("m_lo", [P, FT, SEQ], F32R)
        w_raw = n.sb("w_raw", [P, 2, QUART, HALF])
        w_hi, w_lo = n.sb("w_hi", [P, 2, QUART, HALF], F32R), n.sb("w_lo", [P, 2, QUART, HALF], F32R)
        res, x_in = n.sb("res", [P, GROUP, HALF]), n.sb("x_in", [P, GROUP, HALF])
        m_raw = w_raw[:].rearrange("p b q n -> p (b q n)").rearrange("p (b s) -> p b s", s=SEQ)
        acc = n.ps("acc", [P, 2, GROUP, HALF])
        l_m = [n.sem(f"l_m{i}") for i in range(4)]
        l_w = [n.sem(f"l_w{i}") for i in range(2)]
        m_h, m_l, w_h, w_l, used, acc_done, left, l_x, o_r = (
            n.sem(x_) for x_ in ("m_h", "m_l", "w_h", "w_l", "used", "acc_done", "left", "l_x", "o_r"))
        st = n.sem("st")
        block = stack.enter_context(nc.Block())
        ONE = 1
        KU = NQ - 1

        @block.sync
        def _(sp):
            for f in range(FT):
                if f >= 4:
                    sp.wait_ge(m_l, f - 3)
                sp.dma_start(m_raw[:, f % 4], mixed[f]).then_inc(l_m[f % 4], 16)

            def load(sl, q, wait):
                wait()
                sp.dma_start(w_raw[:, q % 2], w_out[bass.ds(sl, 1), :, QUART * HALF * q:QUART * HALF * (q + 1)]
                             .rearrange("a p (q n) -> p (a q) n", n=HALF)).then_inc(l_w[q % 2], 16)

            def step(i, g, first):
                for q in range(NQ):
                    if first and q < 2:
                        load(i, q, lambda: sp.wait_ge(m_l, FT))
                    else:
                        load(i, q, lambda: sp.wait_ge(w_l, i * (2 * NQ) + (g * NQ + q - 1)))
                if not first:
                    sp.wait_ge(o_r, i * (2 * GROUP) + g * GROUP)
                sp.dma_start(x_in[:], x[GROUP * P * g:GROUP * P * (g + 1), bass.ds(i * HALF, HALF)]
                             .rearrange("(a p) n -> p a n", p=P)).then_inc(l_x, 16)

            step(0, 0, True)
            step(0, 1, False)
            with sp.Fori(1, NS) as i:
                step(i, 0, False)
                step(i, 1, False)

        @block.scalar
        def _(act):
            for f in range(FT):
                act.wait_ge(l_m[f % 4], 16 * (f // 4 + 1))
                act.activation(m_hi[:, f], m_raw[:, f % 4], ACT.Copy).then_inc(m_h, 1)
            with act.Fori(0, NS) as i:
                for g in range(2):
                    for q in range(NQ):
                        act.wait_ge(l_w[q % 2], i * (16 * NQ) + 16 * (g * (NQ // 2) + q // 2 + 1))
                        if q == 1:
                            act.wait_ge(acc_done, i * (2 * GROUP) + (g * GROUP + ONE))
                        else:
                            act.wait_ge(used, i * (2 * KU) + (g * KU + max(q - 1, 0) + ONE))
                        act.activation(w_hi[:, q % 2], w_raw[:, q % 2], ACT.Copy).then_inc(w_h, 1)

        @block.gpsimd
        def _(pool):
            with pool.Fori(0, NS) as i:
                for g in range(2):
                    pool.wait_ge(o_r, i * (2 * GROUP) + (g + 1) * GROUP)
                    pool.dma_start(out[GROUP * P * g:GROUP * P * (g + 1), bass.ds(i * HALF, HALF)]
                                   .rearrange("(a p) n -> p a n", p=P), res[:]).then_inc(st, 16)
                    pool.wait_ge(st, i * 32 + 16 * (g + 1))
                    pool.sem_inc(left, 1)

        @block.vector
        def _(dve):
            for f in range(FT):
                dve.wait_ge(m_h, f + 1)
                dve.tensor_tensor(m_lo[:, f], m_raw[:, f % 4], m_hi[:, f].bitcast(F32), ALU.subtract).then_inc(m_l, 1)

            def low(i, g, q):
                dve.wait_ge(w_h, i * (2 * NQ) + (g * NQ + q + 1))
                dve.tensor_tensor(w_lo[:, q % 2], w_raw[:, q % 2], w_hi[:, q % 2].bitcast(F32),
                                  ALU.subtract).then_inc(w_l, 1)

            def finish(i, g, first):
                if not first:
                    dve.wait_ge(left, i * 2 + g)
                dve.wait_ge(l_x, i * 32 + 16 * (g + 1))
                for a in range(GROUP):
                    dve.wait_ge(acc_done, i * (2 * GROUP) + (g * GROUP + a + 1 + ONE))
                    dve.tensor_tensor(res[:, a], acc[:, g, a], x_in[:, a], ALU.add).then_inc(o_r, 1)

            low(0, 0, 0)
            low(0, 0, 1)

            def step(i, g, first, last):
                for q in range(2, NQ):
                    low(i, g, q)
                if not last:
                    low(i if g == 0 else i + 1, 1 - g, 0)
                finish(i, g, first)
                if not last:
                    low(i if g == 0 else i + 1, 1 - g, 1)

            step(0, 0, True, False)
            step(0, 1, False, False)
            with dve.Fori(1, NS - 1) as i:
                step(i, 0, False, False)
                step(i, 1, False, False)
            step(NS - 1, 0, False, False)
            step(NS - 1, 1, False, True)

        @block.tensor
        def _(pe):
            pe.sem_inc(used, ONE)
            pe.sem_inc(acc_done, ONE)
            pe.wait_ge(m_h, FT)
            pe.wait_ge(m_l, FT)

            def step(i, g, free):
                for q in range(NQ):
                    pe.wait_ge(w_h, i * (2 * NQ) + (g * NQ + q + 1))
                    pe.wait_ge(w_l, i * (2 * NQ) + (g * NQ + q + 1))
                    if q == 0 and not free:
                        pe.wait_ge(o_r, i * (2 * GROUP) + (g * GROUP - GROUP))
                    for a in range(GROUP):
                        rows = bass.ts(g * GROUP + a, P)
                        for k in range(QUART):
                            f = QUART * q + k
                            last = split_product(pe, acc[:, g, a], m_hi[:, f, rows], m_lo[:, f, rows],
                                                 w_hi[:, q % 2, k], w_lo[:, q % 2, k], f == 0, f == FT - 1)
                        if q == NQ - 1:
                            last.then_inc(acc_done, 1)
                    if q < NQ - 1:
                        last.then_inc(used, 1)

            step(0, 0, True)
            step(0, 1, True)
            with pe.Fori(1, NS) as i:
                step(i, 0, False)
                step(i, 1, False)


def program(nc, args, out):
    proj = nc.dram_tensor("proj_scratch", (TILES, P, SEQ), F32, kind=args.get("kind", "Internal")).ap()
    kv_scratch = nc.dram_tensor("kv_scratch", (P, 2, 2, HALF), F32, kind="Internal").ap()
    gate_rows = nc.dram_tensor("gate_rows", (4, A_HEADS, SEQ), F32, kind="Internal").ap()
    mixed = nc.dram_tensor("mixed_scratch", (D_MODEL // P, P, SEQ), F32, kind=args.get("kind", "Internal")).ap()
    with ExitStack() as stack:
        n = Names(nc, stack, "c_")
        c = {"ones": n.sb("ones", [P, P])}
        values = {"one": 1.0, "eps": EPS, "eps4": 4 * EPS, "eps64": 64 * EPS, "eps128": 128 * EPS}
        for name in values:
            c[name] = n.sb(name, [P, 1])
        with nc.Block() as block:
            @block.vector
            def _(dve):
                dve.memset(c["ones"][:], 1.0)
                for name, value in values.items():
                    dve.memset(c[name][:], value)

        memory_stage(nc, c, args["mem_t"], args["mem_norm_w"], args["w_mem"], args["k_norm_c"], kv_scratch)
        with ExitStack() as held:
            x_hi = held.enter_context(nc.sbuf_tensor("x_hi", [P, KT, SEQ], F32R))
            x_lo = held.enter_context(nc.sbuf_tensor("x_lo", [P, KT, SEQ], F32R))
            input_norm_stage(nc, c, args["x_t"], args["norm_w"], x_hi, x_lo)
            projection_stage(nc, c, args["w_in"], args["conv_w"], x_hi, x_lo, proj)
        cols = n.sb("cols", [P, 4, A_HEADS, NC])
        shapes = {"ident": [P, P], "neg": [P, 2, P], "level1": [P, 2, P], "masks": [P, len(LEVELS), P]}
        s_const = n.sem("s_const")
        for name in shapes:
            c[name] = n.sb(name, shapes[name])
        with nc.Block() as block:
            @block.sync
            def _(sp):
                for name in shapes:
                    sp.dma_start(c[name][:], args[name]).then_inc(s_const, 16)
                sp.wait_ge(s_const, 64)

        gate_stage(nc, c, proj, args["gate_consts"], gate_rows, cols)
        delta_stage(nc, c, proj, gate_rows, cols, args["o_norm"], mixed)
        attention_stage(nc, c, proj, kv_scratch, args, mixed)
        output_stage(nc, c, mixed, args["w_out"], args["x"], out)


def shape_constants():
    row, col = np.meshgrid(np.arange(P), np.arange(P), indexing="ij")
    f = np.float32

    def both(fwd, bwd):
        return np.ascontiguousarray(np.stack([fwd, bwd], 1).astype(f))

    same2 = row // 2 == col // 2
    levels = []
    for s in LEVELS:
        same = row // (2 * s) == col // (2 * s)
        levels.append((same & (row // s != col // s)).astype(f))
    key = np.arange(3 * P)[None, :]
    i = np.arange(P)[:, None]
    band = (key >= i) & (key <= i + 2 * WINDOW)
    window = np.stack([np.where(m, f(0), f(NEG)) for m in (band & (key >= P), band, band & (key < 2 * P))], 1)
    half = B_DIM // 2
    rot = np.zeros((P, P), f)
    for p in range(P):
        if p % B_DIM < half:
            rot[p + half, p] = -1
        else:
            rot[p - half, p] = 1
    inv = f(10000.0) ** (-np.arange(0, B_DIM, 2, dtype=f) / f(B_DIM))
    angle = inv[np.arange(P) % half][:, None] * np.arange(SEQ, dtype=f)[None, :]
    return {
        "ident": np.eye(P, dtype=f),
        "neg": both(np.where(col >= row, f(0), f(NEG)), np.where(col <= row, f(0), f(NEG))),
        "level1": both(same2 & (col % 2 == 1) & (row % 2 == 0), same2 & (col % 2 == 0) & (row % 2 == 1)),
        "masks": np.ascontiguousarray(np.stack(levels, 1)),
        "cos": np.cos(angle), "sin": np.sin(angle), "rot": rot, "window": np.ascontiguousarray(window),
        "half_ones": (row[:, :2] // B_DIM == col[:, :2]).astype(f),
        "pair_ones": (row // B_DIM == col // B_DIM).astype(f),
    }


def lay_out(x, mem, norm_w, w_in, conv_w_a, a_log_fwd, a_log_bwd, dt_bias_fwd, dt_bias_bwd, o_norm_a, q_norm_b,
            k_norm_b, sink_b, mem_norm_w, w_mem_kv, q_norm_c, k_norm_c, w_out):
    A, B = A_HEADS * P, B_HEADS * B_DIM
    tile = np.arange(P)
    b_tiles = [np.concatenate([np.arange(B_DIM) + B_DIM * j, np.arange(B_DIM) + B_DIM * (j + 4)]) for j in range(4)]
    gates, b0 = 4 * A, 4 * A + 4 * A_HEADS
    bk, bz, c0 = b0 + B, b0 + B + 2 * P, b0 + 2 * B + 2 * P
    cols = [part * A + h * P + tile for h in range(A_HEADS) for part in range(4)]
    cols += [b0 + t for t in b_tiles] + [bk + tile, bk + P + tile] + [bz + t for t in b_tiles]
    cols += [c0 + C_HEADS * P + j * P + tile for j in range(4)] + [c0 + j * P + tile for j in range(4)]

    w = w_in[0].reshape(KT, P, -1)
    w_tiles = np.zeros((TILES, P, KT, P), np.float32)
    for t, where in enumerate(cols):
        w_tiles[t] = w[:, :, where].transpose(1, 0, 2)
    gate_consts = np.zeros((P, 2), np.float32)
    for g, (dt_bias, a_log) in enumerate(((dt_bias_fwd, a_log_fwd), (dt_bias_bwd, a_log_bwd))):
        gate_consts[32 * g:32 * g + A_HEADS, 0] = dt_bias[0]
        gate_consts[32 * g:32 * g + A_HEADS, 1] = a_log[0]
    for g in range(4):
        where = slice(gates + A_HEADS * g, gates + A_HEADS * (g + 1))
        w_tiles[T_GATE][:, :, 32 * g:32 * g + A_HEADS] = w[:, :, where].transpose(1, 0, 2)

    def features(a):
        return np.ascontiguousarray(a.T.reshape(KT, P, -1).transpose(1, 0, 2))

    rows = [np.arange(A)] + [A + t for t in b_tiles] + [A + B + np.arange(C_HEADS * P)]
    w_o = w_out[0][np.concatenate(rows)].reshape(KT, P, D_MODEL // HALF, HALF)
    out = {
        "x": x[0], "x_t": features(x[0]), "mem_t": features(mem[0]),
        "norm_w": norm_w[0].reshape(KT, P).T, "mem_norm_w": mem_norm_w[0].reshape(KT, P).T,
        "w_in": w_tiles.reshape(TILES, P, KT * P),
        "w_mem": w_mem_kv[0].reshape(KT, P, -1).transpose(1, 0, 2),
        "w_out": w_o.transpose(2, 1, 0, 3).reshape(D_MODEL // HALF, P, KT * HALF),
        "conv_w": conv_w_a[0].reshape(CONV_K, 3, A_HEADS, P).transpose(3, 2, 1, 0).reshape(P, -1),
        "gate_consts": gate_consts, "o_norm": o_norm_a[0][:, None], "k_norm_c": k_norm_c[0],
        "qw": np.concatenate([q_norm_b[0]] * 2)[:, None], "kw": np.concatenate([k_norm_b[0]] * 2)[:, None],
        "cw": q_norm_c[0][:, None], "sink": np.repeat(sink_b[0].reshape(1, 2, 4), P, 0),
    }
    return {k: np.ascontiguousarray(v) for k, v in out.items()}


def kernel(**inputs):
    import concourse.bacc as bacc
    from concourse.bass_utils import run_bass_kernel_spmd

    arrays = lay_out(**{k: np.asarray(v) for k, v in inputs.items()}) | shape_constants()
    nc = bacc.Bacc("TRN2", target_bir_lowering=False, num_devices=1)
    args = {k: nc.dram_tensor("in_" + k, a.shape, mybir.dt.from_np(a.dtype), kind="ExternalInput").ap()
            for k, a in arrays.items()}
    out = nc.dram_tensor("out", (SEQ, D_MODEL), F32, kind="ExternalOutput").ap()
    program(nc, args, out)
    r = run_bass_kernel_spmd(nc, [{"in_" + k: a for k, a in arrays.items()}], core_ids=[0])
    return r.results[0]["out"].reshape(1, SEQ, D_MODEL)
```
